# Optimizing a Trainium2 kernel written in Bass

```python
import math
import jax, jax.numpy as jnp
from jax import lax
import numpy as np

D_MODEL = 1024
BATCH = 1
SEQ = 256
DEPTH = 1

ATTN_GROUPS = ((128, 1), (512, 4), (2048, 16))
N_ATTN_GROUPS = len(ATTN_GROUPS)
ATTN_HEADS = 8
ATTN_HEAD_DIM = D_MODEL // 16
ATTN_GROUP_WIDTH = ATTN_HEADS * ATTN_HEAD_DIM
ATTN_QKV_WIDTH = N_ATTN_GROUPS * ATTN_GROUP_WIDTH
RET_HEADS = 4
RET_KEY_DIM = D_MODEL // 8
RET_VALUE_DIM = 2 * RET_KEY_DIM
RET_QK_WIDTH = RET_HEADS * RET_KEY_DIM
RET_V_WIDTH = RET_HEADS * RET_VALUE_DIM
RET_CHUNK = 128
N_BRANCHES = 2
IN_SPLITS = (ATTN_QKV_WIDTH, ATTN_QKV_WIDTH, ATTN_QKV_WIDTH,
             RET_QK_WIDTH, RET_QK_WIDTH, RET_V_WIDTH, RET_V_WIDTH,
             D_MODEL, D_MODEL)
IN_WIDTH = sum(IN_SPLITS)
N_EXPERT_GROUPS = 4
EXPERTS_PER_GROUP = 8
N_EXPERTS = N_EXPERT_GROUPS * EXPERTS_PER_GROUP
TOP_K_IN_GROUP = 2
EXPERT_FF = D_MODEL // 2
EPS = 1e-6

kernel_name = "hybrid_dilated_attn_retention_hmoe_block"

def rms_norm(x, g):
    xf = x.astype(jnp.float32)
    y = xf * lax.rsqrt(jnp.mean(xf * xf, axis=-1, keepdims=True) + EPS)
    return (y * g.astype(jnp.float32)).astype(x.dtype)

def alibi_slopes(n):
    return jnp.exp2(-8.0 * jnp.arange(1, n + 1, dtype=jnp.float32) / n)

def dilated_window_attention(q, k, v, slopes, window, dilation):
    B, S, H, Dh = q.shape
    n_back = window // dilation
    blk = n_back
    L = S // dilation
    nb = -(-L // blk)
    Lp = nb * blk

    def to_blocks(t):
        t = t.reshape(B, L, dilation, H, Dh)
        t = jnp.pad(t, ((0, 0), (0, Lp - L), (0, 0), (0, 0), (0, 0)))
        t = t.reshape(B, nb, blk, dilation, H, Dh)
        return t.transpose(0, 3, 4, 1, 2, 5)

    def with_prev(t):
        prev = jnp.pad(t, ((0, 0), (0, 0), (0, 0), (1, 0), (0, 0), (0, 0)))[:, :, :, :-1]
        return jnp.concatenate([prev, t], axis=4)

    qb, kb, vb = to_blocks(q), to_blocks(k), to_blocks(v)
    kk, vv = with_prev(kb), with_prev(vb)
    s = jnp.einsum('brhnqc,brhnkc->brhnqk', qb, kk,
                   preferred_element_type=jnp.float32) * (Dh ** -0.5)
    qi = jnp.arange(blk)[:, None]
    kj = jnp.arange(2 * blk)[None, :]
    rel = qi + blk - kj
    blk_idx = jnp.arange(nb)[:, None, None]
    valid = (rel >= 0) & (rel <= n_back) & ((blk_idx > 0) | (kj >= blk))
    bias = -slopes[:, None, None, None] * (rel * dilation).astype(jnp.float32)
    s = jnp.where(valid, s + bias, -jnp.inf)
    m = jnp.max(s, axis=-1, keepdims=True)
    p = jnp.exp(s - m)
    den = jnp.sum(p, axis=-1, keepdims=True)
    o = jnp.einsum('brhnqk,brhnkc->brhnqc', p, vv.astype(jnp.float32)) / den
    lse = (m + jnp.log(den))[..., 0]
    o = o.transpose(0, 3, 4, 1, 2, 5).reshape(B, Lp, dilation, H, Dh)[:, :L]
    lse = lse.transpose(0, 3, 4, 1, 2).reshape(B, Lp, dilation, H)[:, :L]
    return o.reshape(B, S, H, Dh), lse.reshape(B, S, H)

def retention_chunkwise(q, k, v):
    B, S, H, Dk = q.shape
    Dv = v.shape[-1]
    C = RET_CHUNK
    nc = S // C
    log_g = jnp.log1p(-jnp.exp2(-5.0 - jnp.arange(H, dtype=jnp.float32)))
    pos = jnp.arange(C, dtype=jnp.float32)
    diff = pos[:, None] - pos[None, :]
    decay_in = jnp.where(diff >= 0, jnp.exp(log_g[:, None, None] * jnp.maximum(diff, 0.0)), 0.0)
    xi = jnp.exp(log_g[:, None] * (pos + 1.0))[..., None]
    zeta = jnp.exp(log_g[:, None] * (C - 1.0 - pos))[..., None]
    g_chunk = jnp.exp(log_g * C)[:, None, None]

    def chunks(t):
        return t.astype(jnp.float32).reshape(B, nc, C, H, t.shape[-1]).transpose(1, 0, 3, 2, 4)

    qc, kc, vc = chunks(q), chunks(k) * (Dk ** -0.5), chunks(v)

    def step(state, inp):
        qi, ki, vi = inp
        att = jnp.einsum('bhqd,bhkd->bhqk', qi, ki) * decay_in
        inner = jnp.einsum('bhqk,bhkv->bhqv', att, vi)
        cross = jnp.einsum('bhqd,bhdv->bhqv', qi, state) * xi
        state = g_chunk * state + jnp.einsum('bhkd,bhkv->bhdv', ki * zeta, vi)
        return state, inner + cross

    state0 = jnp.zeros((B, H, Dk, Dv), jnp.float32)
    _, y = lax.scan(step, state0, (qc, kc, vc))
    return y.transpose(1, 0, 3, 2, 4).reshape(B, S, H, Dv)

def hier_moe(h, w_gr, b_gr, w_er, b_er, w_gate, w_up, w_down):
    N = h.shape[0]
    g_prob = jax.nn.softmax((h @ w_gr + b_gr).astype(jnp.float32), axis=-1)
    g_val, g_idx = lax.top_k(g_prob, 1)
    g_onehot = jax.nn.one_hot(g_idx[:, 0], N_EXPERT_GROUPS, dtype=jnp.float32)
    e_logit = (h @ w_er + b_er).astype(jnp.float32).reshape(N, N_EXPERT_GROUPS, EXPERTS_PER_GROUP)
    e_sel = jnp.einsum('nge,ng->ne', e_logit, g_onehot)
    e_val, e_idx = lax.top_k(e_sel, TOP_K_IN_GROUP)
    e_w = jax.nn.softmax(e_val, axis=-1)
    e_gate = jnp.sum(e_w[..., None] * jax.nn.one_hot(e_idx, EXPERTS_PER_GROUP, dtype=jnp.float32), axis=1)
    gate = (g_val[:, 0:1] * g_onehot)[:, :, None] * e_gate[:, None, :]
    wg = w_gate.reshape(N_EXPERT_GROUPS, EXPERTS_PER_GROUP, D_MODEL, EXPERT_FF)
    wu = w_up.reshape(N_EXPERT_GROUPS, EXPERTS_PER_GROUP, D_MODEL, EXPERT_FF)
    wd = w_down.reshape(N_EXPERT_GROUPS, EXPERTS_PER_GROUP, EXPERT_FF, D_MODEL)
    y = jnp.zeros((N, D_MODEL), jnp.float32)
    for grp in range(N_EXPERT_GROUPS):
        a = jnp.einsum('nd,edf->enf', h, wg[grp])
        u = jnp.einsum('nd,edf->enf', h, wu[grp])
        hid = jax.nn.silu(a) * u * gate[:, grp].T[:, :, None]
        y = y + jnp.einsum('enf,efd->nd', hid, wd[grp])
    return y

def setup_inputs(seed: int = 0) -> dict:
    key = jax.random.key(seed)
    ks = jax.random.split(key, 16)
    f32 = jnp.float32
    nrm = lambda k, shape, fan_in: jax.random.normal(k, shape, f32) * (fan_in ** -0.5)
    gain = lambda k, shape: 1.0 + 0.01 * jax.random.normal(k, shape, f32)
    return {
        "x": jax.random.normal(ks[0], (BATCH, SEQ, D_MODEL), f32),
        "g_mix": gain(ks[1], (DEPTH, D_MODEL)),
        "w_in": nrm(ks[2], (DEPTH, D_MODEL, IN_WIDTH), D_MODEL),
        "w_attn_branch": nrm(ks[3], (DEPTH, ATTN_GROUP_WIDTH, D_MODEL), ATTN_GROUP_WIDTH),
        "w_ret_branch": nrm(ks[4], (DEPTH, RET_V_WIDTH, D_MODEL), RET_V_WIDTH),
        "w_out": nrm(ks[5], (DEPTH, D_MODEL, D_MODEL), D_MODEL),
        "g_ffn": gain(ks[6], (DEPTH, D_MODEL)),
        "w_group_router": nrm(ks[7], (DEPTH, D_MODEL, N_EXPERT_GROUPS), D_MODEL),
        "b_group_router": 0.01 * jax.random.normal(ks[8], (DEPTH, N_EXPERT_GROUPS), f32),
        "w_expert_router": nrm(ks[9], (DEPTH, D_MODEL, N_EXPERTS), D_MODEL),
        "b_expert_router": 0.01 * jax.random.normal(ks[10], (DEPTH, N_EXPERTS), f32),
        "w_gate": nrm(ks[11], (DEPTH, N_EXPERTS, D_MODEL, EXPERT_FF), D_MODEL),
        "w_up": nrm(ks[12], (DEPTH, N_EXPERTS, D_MODEL, EXPERT_FF), D_MODEL),
        "w_down": nrm(ks[13], (DEPTH, N_EXPERTS, EXPERT_FF, D_MODEL), EXPERT_FF),
        "g_final": gain(ks[14], (D_MODEL,)),
    }

def reference(x, g_mix, w_in, w_attn_branch, w_ret_branch, w_out, g_ffn,
              w_group_router, b_group_router, w_expert_router, b_expert_router,
              w_gate, w_up, w_down, g_final):
    B, S, D = x.shape
    slopes = alibi_slopes(ATTN_HEADS)
    split_at = np.cumsum(np.array(IN_SPLITS))[:-1].tolist()
    for layer in range(DEPTH):
        h = rms_norm(x, g_mix[layer])
        proj = h @ w_in[layer]
        qa, ka, va, qr, kr, vr, gr_swish, gate_a, gate_r = jnp.split(proj, split_at, axis=-1)
        qa = qa.reshape(B, S, N_ATTN_GROUPS, ATTN_HEADS, ATTN_HEAD_DIM)
        ka = ka.reshape(B, S, N_ATTN_GROUPS, ATTN_HEADS, ATTN_HEAD_DIM)
        va = va.reshape(B, S, N_ATTN_GROUPS, ATTN_HEADS, ATTN_HEAD_DIM)
        outs, lses = [], []
        for gi, (window, dilation) in enumerate(ATTN_GROUPS):
            o, l = dilated_window_attention(qa[:, :, gi], ka[:, :, gi], va[:, :, gi],
                                            slopes, window, dilation)
            outs.append(o)
            lses.append(l)
        mix_w = jax.nn.softmax(jnp.stack(lses, axis=0), axis=0)
        o_attn = jnp.einsum('gbsh,gbshc->bshc', mix_w, jnp.stack(outs, axis=0))
        o_attn = o_attn.reshape(B, S, ATTN_GROUP_WIDTH).astype(x.dtype)

        yr = retention_chunkwise(qr.reshape(B, S, RET_HEADS, RET_KEY_DIM),
                                 kr.reshape(B, S, RET_HEADS, RET_KEY_DIM),
                                 vr.reshape(B, S, RET_HEADS, RET_VALUE_DIM))
        mu = jnp.mean(yr, axis=-1, keepdims=True)
        var = jnp.mean(jnp.square(yr - mu), axis=-1, keepdims=True)
        yr = ((yr - mu) * lax.rsqrt(var + EPS)).reshape(B, S, RET_V_WIDTH)
        o_ret = (jax.nn.silu(gr_swish.astype(jnp.float32)) * yr).astype(x.dtype)

        merged = (jax.nn.sigmoid(gate_a) * (o_attn @ w_attn_branch[layer])
                  + jax.nn.sigmoid(gate_r) * (o_ret @ w_ret_branch[layer]))
        x = x + merged @ w_out[layer]

        h2 = rms_norm(x, g_ffn[layer]).reshape(B * S, D)
        y = hier_moe(h2, w_group_router[layer], b_group_router[layer],
                     w_expert_router[layer], b_expert_router[layer],
                     w_gate[layer], w_up[layer], w_down[layer])
        x = x + y.reshape(B, S, D).astype(x.dtype)
    return rms_norm(x, g_final)


_drawn_inputs = setup_inputs


def setup_inputs(seed=0):
    import zlib

    import numpy as np

    out = dict(_drawn_inputs(seed))
    spreads = {}
    factors = {'b_group_router': 3.907, 'b_expert_router': 8.0, 'g_final': 33.124, 'g_ffn': 3.133}
    for name, (base, spread) in spreads.items():
        noise = np.random.default_rng([zlib.crc32(name.encode()), seed]).standard_normal(out[name].shape)
        drawn = base * np.exp(spread * noise) if base else spread * noise
        out[name] = __import__('jax').numpy.asarray(drawn.astype(out[name].dtype))
    for name, factor in factors.items():
        out[name] = (out[name] * factor).astype(out[name].dtype)
    return out
```

```python
from contextlib import ExitStack

import numpy as np

import concourse.bass as bass
from concourse import mybir

ALU = mybir.AluOpType
ACT = mybir.ActivationFunctionType
AX_X = mybir.AxisListType.X
F32 = mybir.dt.float32
I32 = mybir.dt.int32

P = 128
GROUPS = ((128, 1), (512, 4), (2048, 16))
HEADS = 8
HEAD_DIM = 64
RET_HEADS = 4
N_GROUPS = 4
PER_GROUP = 8
EPS = 1e-6
SLOTS = 64
MASKED = -1e30
RING = 6


def load_weights(sp, sem, out, in_):
    sp.dma_start(out, in_).then_inc(sem, 16)


def chain(eng, sem, base):
    count = [0]

    def link(ins):
        count[0] += 1
        ins.then_inc(sem, 1)
        eng.wait_ge(sem, base + count[0])

    return link, count


def hybrid_block(nc, x, g_mix, w_in, w_attn, w_ret, w_out, g_ffn, w_router, b_router,
                 w_gate, w_up, w_down, g_final, out):
    T, D = x.shape
    TT = T // P
    KT = D // P
    NG = len(GROUPS)
    AW = HEADS * HEAD_DIM
    RK = D // 8
    RV = 2 * RK
    E, _, FF = w_gate.shape
    FT = FF // P
    NP = E // 2
    PAIRS = HEADS // 2
    NR = N_GROUPS + E
    ROUNDS = T // SLOTS
    HALF = D // 2
    assert TT == 2 and KT == 8 and RK == P and HALF == 512 and FT * P == 512 and E == N_GROUPS * PER_GROUP

    COL_Q, COL_K, COL_V = 0, NG * AW, 2 * NG * AW
    COL_RQ = 3 * NG * AW
    COL_RK = COL_RQ + RET_HEADS * RK
    COL_RV = COL_RK + RET_HEADS * RK
    COL_RG = COL_RV + RET_HEADS * RV
    COL_GA = COL_RG + RET_HEADS * RV
    COL_GR = COL_GA + D
    w_in_v = w_in.rearrange("(p k) n -> p k n", k=KT)
    wattn_v = w_attn.rearrange("(c p) n -> p c n", p=P)
    wret_v = w_ret.rearrange("(c p) n -> p c n", p=P)
    wout_v = w_out.rearrange("(c p) n -> p c n", p=P)
    wg_v = w_gate.rearrange("e (p k) f -> e p (k f)", k=KT)
    wu_v = w_up.rearrange("e (p k) f -> e p (k f)", k=KT)
    wd_v = w_down.rearrange("e (c p) d -> e p c d", p=P)
    x_v = x.rearrange("(a p) d -> p a d", p=P)
    out_v = out.rearrange("(a p) d -> p a d", p=P)

    with ExitStack() as ctx:
        def sb(name, shape, dt=F32):
            return ctx.enter_context(nc.sbuf_tensor(name, shape, dt))

        def sem(name):
            return ctx.enter_context(nc.semaphore(name))

        ps = ctx.enter_context(nc.psum_tensor("ps", [P, 8, 512], F32))

        ring = sb("ring", [P, RING, 4096])
        xs = sb("xs", [P, TT, D])
        hn = sb("hn", [P, TT, KT, P])
        hT = sb("hT", [P, KT, T])
        g1 = sb("g1", [P, D])
        g2 = sb("g2", [P, D])
        g3 = g1
        ident = sb("ident", [P, P])
        before = sb("before", [P, P])
        ones = sb("ones", [P, P])
        bias_t = sb("bias_t", [P, NG, T])
        slope = sb("slope", [P, 2])
        decay = sb("decay", [P, RET_HEADS, 3 * P])
        age = sb("age", [P, 3 * P])
        half_neg = sb("half_neg", [P, 2])
        slot_ids = sb("slot_ids", [P, ROUNDS * SLOTS])
        rev_ids = sb("rev_ids", [P, NR])
        ss = sb("ss", [P, 3, TT])
        ms = sb("ms", [P, 3, TT])
        rstd = sb("rstd", [P, 3, TT])

        mid = sb("mid", [P, 2 * KT * T])
        qT = mid[:, 0:NG * T].rearrange("p (g t) -> p g t", g=NG)
        kT = mid[:, NG * T:2 * NG * T].rearrange("p (g t) -> p g t", g=NG)
        vA = mid[:, 2 * NG * T:2 * NG * T + TT * NG * P].rearrange("p (a g n) -> p a g n", a=TT, g=NG)
        gateA = mid[:, 0:KT * T].rearrange("p (k t) -> p k t", k=KT)
        gateR = mid[:, KT * T:2 * KT * T].rearrange("p (k t) -> p k t", k=KT)
        UC = [NG * T, NG * P]
        work = sb("work", [P, 4 * (UC[0] + UC[1])])

        def part(at, n):
            return work[:, at:at + n]

        at_u = [0, UC[0], UC[0] + UC[1], 2 * UC[0] + UC[1]]
        probs = [part(at_u[u], UC[u % 2]) for u in range(4)]
        probsT = [part(2 * (UC[0] + UC[1]) + at_u[u], UC[u % 2]) for u in range(4)]
        negmax = sb("negmax", [P, 4])
        den = sb("den", [P, 4])
        rden = sb("rden", [P, 4])
        oA = sb("oA", [P, TT, P])
        oAT = sb("oAT", [P, PAIRS + 1, T])

        qkR = sb("qkR", [P, 2, T])
        vR = sb("vR", [P, TT, RV])
        attR = sb("attR", [P, 3 * P])
        stats = sb("stats", [P, TT, 6])
        meanvar = sb("meanvar", [P, TT, 2])
        rstdR = sb("rstdR", [P, TT])
        swish = sb("swish", [P, TT, RV])
        oR = sb("oR", [P, TT, RV])
        oRT = sb("oRT", [P, 2 * RET_HEADS + 2, T])

        eG = part(0, 4 * T).rearrange("p (a c t) -> p a c t", a=2, c=2)
        merged = part(4 * T, KT * T).rearrange("p (k t) -> p k t", k=KT)
        mtmp = part((4 + KT) * T, 2 * T).rearrange("p (k t) -> p k t", k=2)
        junk = part(0, D)
        dist_i = part(D, T).bitcast(I32)
        resid_i = part(D + T, T).bitcast(I32)
        resid_f = part(D + 2 * T, T)
        dist = part(D + 3 * T, T)

        wr = sb("wr", [P, KT, NR])
        br = sb("br", [P, NR])
        lg = sb("lg", [P, TT, NR])
        ra = sb("ra", [P, TT, NR])
        rb = sb("rb", [P, TT, NR])
        r1 = sb("r1", [P, 12, TT])
        oh1 = sb("oh1", [P, TT, E])
        oh2 = sb("oh2", [P, TT, E])
        gate = sb("gate", [P, TT, E])
        sel = sb("sel", [P, TT, E])
        sel_all = sb("sel_all", [P, E])
        pos = sb("pos", [P, TT, E])
        cnt = sb("cnt", [1, 4, NP])
        sched_f = sb("sched_f", [1, 3, NP])
        sched = sb("sched", [1, 2, NP], I32)

        onehot = part(3 * KT * P + 4 * FT * SLOTS, TT * P).rearrange("p (a s) -> p a s", a=TT)
        gated = part(3 * KT * P + 4 * FT * SLOTS + TT * P, TT * P).rearrange("p (a s) -> p a s", a=TT)
        gatedT = sb("gatedT", [P, T])
        xg = part(0, KT * P).rearrange("p (k s) -> p k s", k=KT)
        yT = part(KT * P, KT * P).rearrange("p (k s) -> p k s", k=KT)
        yS = part(2 * KT * P, D)
        sg = part(3 * KT * P, 2 * FT * SLOTS).rearrange("p (j s) -> p j s", j=2)
        hid = part(3 * KT * P + 2 * FT * SLOTS, 2 * FT * SLOTS).rearrange("p (j s) -> p j s", j=2)
        res = xs

        s_x = [sem(f"s_x{t}") for t in range(TT)]
        s_g1 = sem("s_g1")
        s_g2 = sem("s_g2")
        s_g3 = sem("s_g3")
        s_wr = sem("s_wr")
        s_w = [sem(f"s_w{i}") for i in range(RING)]
        s_out = sem("s_out")
        const_ready = sem("const_ready")
        pool_chain = sem("pool_chain")
        dve_chain = sem("dve_chain")
        sq_done = sem("sq_done")
        ms_done = sem("ms_done")
        rstd_done = sem("rstd_done")
        hn_done = sem("hn_done")
        hT_psum = sem("hT_psum")
        hT_act = sem("hT_act")
        hT_dve = sem("hT_dve")
        tables = sem("tables")
        age_done = sem("age_done")
        decay_done = sem("decay_done")

        aq_done, ak_done, av_done = sem("aq_done"), sem("ak_done"), sem("av_done")
        aq_ev, ak_ev, av_ev = sem("aq_ev"), sem("ak_ev"), sem("av_ev")
        as_done, as_chain, as_ready = sem("as_done"), sem("as_chain"), sem("as_ready")
        slope_chain = sem("slope_chain")
        ap_ready = sem("ap_ready")
        apt_done, apt_act, apt_dve = sem("apt_done"), sem("apt_act"), sem("apt_dve")
        ao_done, ao_rden, ao_ev = sem("ao_done"), sem("ao_rden"), sem("ao_ev")
        aoT_done, aoT_ev = sem("aoT_done"), sem("aoT_ev")

        rqk_done, rv_done, rg_done = sem("rqk_done"), sem("rv_done"), sem("rg_done")
        rqk_ev, rv_ev = sem("rqk_ev"), sem("rv_ev")
        rat_done, rat_ev = sem("rat_done"), sem("rat_ev")
        ry_done, rvar, rrstd, rexp = sem("ry_done"), sem("rvar"), sem("rrstd"), sem("rexp")
        r_chain, r_out = sem("r_chain"), sem("r_out")
        roT_done, roT_ev = sem("roT_done"), sem("roT_ev")
        rpool, r_stats, r_aggr, r_swish = sem("rpool"), sem("r_stats"), sem("r_aggr"), sem("r_swish")

        g_done, g_exp, g_one, g_ready = sem("g_done"), sem("g_exp"), sem("g_one"), sem("g_ready")
        bA_done, bR_done, bA_ev, b_tmp, b_ready = (sem("bA_done"), sem("bR_done"), sem("bA_ev"),
                                                   sem("b_tmp"), sem("b_ready"))
        wo_done = sem("wo_done")
        logits_done, gexp, e2exp = sem("logits_done"), sem("gexp"), sem("e2exp")
        d_route = sem("d_route")
        sel_ready, pos_done, sched_ready = sem("sel_ready"), sem("pos_done"), sem("sched_ready")

        P_built, Pg_built = sem("P_built"), sem("Pg_built")
        gather_lo, gather_hi = sem("gather_lo"), sem("gather_hi")
        xg_act, xg_dve = sem("xg_act"), sem("xg_dve")
        trY, yS_act, yS_dve = sem("trY"), sem("yS_act"), sem("yS_dve")
        gu_done = [sem(f"gu_done{j}") for j in range(2)]
        silu_done = [sem(f"silu_done{j}") for j in range(2)]
        hid_ready = [sem(f"hid_ready{j}") for j in range(2)]
        down_done = [sem(f"down_done{j}") for j in range(2)]
        scatter_done = sem("scatter_done")
        pgt_done, pgt_ev = sem("pgt_done"), sem("pgt_ev")
        yT_ev = sem("yT_ev")
        fin = sem("fin")

        def slot(s, cols):
            return ring[:, s, 0:KT * cols].rearrange("p (k n) -> p k n", k=KT)

        a_w = [slot(s, NG * P) for s in range(3)]
        r_w = [slot(s, 256) for s in range(3)]
        half_w = [ring[:, s, :].rearrange("p (c n) -> p c n", c=4) for s in range(3)]
        pair_w = [slot(s, FF) for s in range(4)] + [ring[:, s, :].rearrange("p (c n) -> p c n", c=FT)
                                                    for s in (4, 5)]
        WG, WU, WD = (0, 2), (1, 3), (4, 5)

        w_a = [lambda i: 16 * (i + 1)] * 3
        BASE_R = 16 * PAIRS
        w_r = [lambda i: BASE_R + 32 * (i + 1), lambda i: BASE_R + 16 * (i + 1), lambda i: BASE_R + 16 * (i + 1)]
        BASE_G = [BASE_R + 32 * RET_HEADS, BASE_R + 16 * RET_HEADS, BASE_R + 16 * RET_HEADS]
        GI = D // 256
        BASE_B = [BASE_G[0] + 16 * GI, BASE_G[1] + 16 * GI, BASE_G[2]]
        W_ATTN = BASE_B[2] + 16
        W_RET = (BASE_B[0] + 16, BASE_B[1] + 16)
        W_OUT = (BASE_B[2] + 32, BASE_B[0] + 32)
        BASE_E = [BASE_B[0] + 32, BASE_B[1] + 16, BASE_B[2] + 32, 0, 0, 0]

        def bank(b, n=512):
            return ps[:, b, 0:n]

        def s_cols(u):
            return (ps[:, 4:6, :].rearrange("p b n -> p (b n)")[:, 0:UC[0]], bank(6, UC[1]),
                    ps[:, 2:4, :].rearrange("p b n -> p (b n)")[:, 0:UC[0]], bank(7, UC[1]))[u]

        block = ctx.enter_context(nc.Block())

        @block.sync
        def _(sp):
            for t in range(TT):
                sp.dma_start(xs[:, t, :], x_v[:, t, :]).then_inc(s_x[t], 16)
            sp.dma_start(g1[:, :], g_mix.partition_broadcast(P)).then_inc(s_g1, 16)

            def load_attn(i):
                for s, c0 in enumerate((COL_Q, COL_K, COL_V)):
                    src = w_in_v[:, :, c0:c0 + NG * AW].rearrange("p k (g n) -> p k g n", g=NG)
                    if not isinstance(i, int) or i > 0:
                        sp.wait_ge((aq_done, ak_done, av_done)[s], i)
                    sp.dma_start(a_w[s].rearrange("p k (g n) -> p k g n", g=NG),
                                 src[:, :, :, bass.ds(i * P, P)]).then_inc(s_w[s], 16)

            load_attn(0)
            load_weights(sp, s_w[3], ring[:, 3, :], wu_v[1])
            load_weights(sp, s_w[4], pair_w[4], wd_v[0])
            load_weights(sp, s_w[5], pair_w[5], wd_v[1])
            with sp.Fori(1, PAIRS) as i:
                load_attn(i)

            def load_ret(i):
                first = isinstance(i, int)
                for s in range(3):
                    if first:
                        sp.wait_ge((aq_done, ak_done, av_done)[s], PAIRS)
                    else:
                        sp.wait_ge((rqk_done, rg_done, rv_done)[s], i)
                    if s == 0:
                        for h, c0 in enumerate((COL_RQ, COL_RK)):
                            sp.dma_start(r_w[0][:, :, h * RK:(h + 1) * RK],
                                         w_in_v[:, :, bass.ds(c0 + i * RK, RK)]).then_inc(s_w[0], 16)
                    else:
                        c0 = (COL_RG, COL_RV)[s - 1]
                        sp.dma_start(r_w[s], w_in_v[:, :, bass.ds(c0 + i * RV, RV)]).then_inc(s_w[s], 16)

            load_ret(0)
            with sp.Fori(1, RET_HEADS) as i:
                load_ret(i)

            def load_gates(i):
                first = isinstance(i, int)
                for s, c0 in enumerate((COL_GA, COL_GR)):
                    if first:
                        sp.wait_ge((rqk_done, rg_done)[s], RET_HEADS)
                    else:
                        sp.wait_ge(g_done, 2 * i - 1 + s)
                    sp.dma_start(r_w[s], w_in_v[:, :, bass.ds(c0 + i * 256, 256)]).then_inc(s_w[s], 16)

            load_gates(0)
            sp.wait_ge(rv_done, RET_HEADS)
            load_weights(sp, s_w[2], half_w[2], wattn_v)
            with sp.Fori(1, GI) as i:
                load_gates(i)

            for s in range(2):
                sp.wait_ge(g_done, 2 * GI - 1 + s)
                load_weights(sp, s_w[s], half_w[s], wret_v[:, 4 * s:4 * s + 4, :])
            sp.wait_ge(bA_done, KT // 2)
            load_weights(sp, s_w[2], half_w[2], wout_v[:, 0:4, :])
            sp.wait_ge(bR_done, KT // 2)
            load_weights(sp, s_w[0], half_w[0], wout_v[:, 4:8, :])
            load_weights(sp, s_w[1], ring[:, 1, :], wu_v[0])
            sp.wait_ge(wo_done, 1)
            load_weights(sp, s_w[2], ring[:, 2, :], wg_v[1])
            sp.wait_ge(wo_done, 2)
            load_weights(sp, s_w[0], ring[:, 0, :], wg_v[0])

            sp.wait_ge(hn_done, TT)
            sp.dma_start(g3[:, :], g_final.partition_broadcast(P)).then_inc(s_g3, 16)
            sp.wait_ge(sched_ready, 1)
            with sp.Fori(1, NP) as p:
                C = sp.value_load(sched[0:1, 1, bass.ds(p, 1)], min_val=1, max_val=ROUNDS * NP)
                e = 2 * p
                sp.wait_ge(gu_done[0], C)
                sp.dma_start(ring[:, 0, :], wg_v[bass.ds(e, 1), :, :].rearrange("e p n -> (e p) n")).then_inc(s_w[0], 16)
                sp.dma_start(ring[:, 1, :], wu_v[bass.ds(e, 1), :, :].rearrange("e p n -> (e p) n")).then_inc(s_w[1], 16)
                sp.wait_ge(gu_done[1], C)
                sp.dma_start(ring[:, 2, :], wg_v[bass.ds(e + 1, 1), :, :].rearrange("e p n -> (e p) n")).then_inc(s_w[2], 16)
                sp.dma_start(ring[:, 3, :], wu_v[bass.ds(e + 1, 1), :, :].rearrange("e p n -> (e p) n")).then_inc(s_w[3], 16)
                sp.wait_ge(down_done[0], C)
                sp.dma_start(pair_w[4], wd_v[bass.ds(e, 1), :, :, :].rearrange("e p c n -> (e p) c n")).then_inc(s_w[4], 16)
                sp.wait_ge(down_done[1], C)
                sp.dma_start(pair_w[5], wd_v[bass.ds(e + 1, 1), :, :, :].rearrange("e p c n -> (e p) c n")).then_inc(s_w[5], 16)

            for t in range(TT):
                sp.wait_ge(fin, t + 1)
                sp.dma_start(out_v[:, t, :], res[:, t, :]).then_inc(s_out, 16)
            sp.wait_ge(s_out, 16 * TT)

        @block.gpsimd
        def _(pool):
            link, _n = chain(pool, pool_chain, 0)
            link(pool.memset(ident[:, :], 0.0))
            pool.affine_select(out=ident[:, :], in_=ident[:, :], compare_op=ALU.not_equal, fill=1.0, base=0,
                               pattern=[[-1, P]], channel_multiplier=1).then_inc(const_ready, 1)
            pool.memset(half_neg[:, :], -0.5).then_inc(const_ready, 1)
            pool.iota(dist_i[:, :], pattern=[[1, T]], base=-P, channel_multiplier=-1).then_inc(const_ready, 1)
            link(pool.iota(age[:, 0:T], pattern=[[1, T]], base=0, channel_multiplier=-1,
                           allow_small_or_imprecise_dtypes=True))
            link(pool.affine_select(out=age[:, 0:P], in_=age[:, 0:P], compare_op=ALU.is_ge, fill=-MASKED, base=0,
                                    pattern=[[1, P]], channel_multiplier=-1))
            pool.tensor_copy(age[:, T:T + P], age[:, 0:P]).then_inc(age_done, 1)

            def inv_root(n):
                pool.wait_ge(ms_done, n + 1)
                pool.tensor_tensor(out=rstd[:, n, :], in0=ms[:, n, :], in1=half_neg[:, 0:TT],
                                   op=ALU.pow).then_inc(rstd_done, 1)

            inv_root(0)
            link(pool.memset(before[:, :], 1.0))
            pool.affine_select(out=before[:, :], in_=before[:, :], compare_op=ALU.is_gt, fill=0.0, base=0,
                               pattern=[[1, P]], channel_multiplier=-1).then_inc(const_ready, 1)
            pool.memset(ones[:, :], 1.0).then_inc(const_ready, 1)
            pool.iota(slot_ids[:, :], pattern=[[1, ROUNDS * SLOTS]], base=0, channel_multiplier=0,
                      allow_small_or_imprecise_dtypes=True).then_inc(const_ready, 1)
            pool.iota(rev_ids[:, :], pattern=[[-1, NR]], base=NR, channel_multiplier=0,
                      allow_small_or_imprecise_dtypes=True).then_inc(const_ready, 1)
            with pool.Fori(0, RET_HEADS) as i:
                pool.wait_ge(rvar, i + 1)
                pool.tensor_tensor(out=rstdR[:, :], in0=meanvar[:, :, 1], in1=half_neg[:, 0:TT],
                                   op=ALU.pow).then_inc(rrstd, 1)
            inv_root(1)
            inv_root(2)

        @block.scalar
        def _(act):
            act.dma_start(g2[:, :], g_ffn.partition_broadcast(P)).then_inc(s_g2, 16)
            act.dma_start(wr[:, :, :], w_router.rearrange("(p k) n -> p k n", k=KT)).then_inc(s_wr, 16)
            act.dma_start(br[:, :], b_router.partition_broadcast(P)).then_inc(s_wr, 16)
            act.sem_inc(aoT_ev, 1)
            act.sem_inc(roT_ev, 1)
            act.sem_inc(g_exp, 2)

            for t in range(TT):
                act.wait_ge(s_x[t], 16)
                if t > 0:
                    act.wait_ge(sq_done, t)
                act.activation(junk[:, :], xs[:, t, :], ACT.Square, accum_out=ss[:, 0, t:t + 1]).then_inc(sq_done, 1)

            def hT_copy(n):
                act.wait_ge(hT_psum, 2 * n + 1)
                act.activation(hT[:, 0:4, :], ps[:, 0:2, :].rearrange("p b (k t) -> p (b k) t", k=2),
                               ACT.Copy).then_inc(hT_act, 1)

            hT_copy(0)
            act.wait_ge(age_done, 1)
            for h in range(RET_HEADS):
                act.activation(decay[:, h, :], age[:, :], ACT.Exp,
                               scale=float(np.log1p(-2.0 ** (-5.0 - h)))).then_inc(decay_done, 1)

            with act.Fori(0, PAIRS) as i:
                act.wait_ge(aq_done, i + 1)
                act.activation(qT[:, :, :].rearrange("p g t -> p (g t)"),
                               ps[:, 0:2, :].rearrange("p b n -> p (b n)")[:, 0:NG * T],
                               ACT.Copy, scale=float(HEAD_DIM) ** -0.5).then_inc(aq_ev, 1)
                act.wait_ge(aoT_done, i + 1)
                act.activation(oAT[:, bass.ds(i, 1), :].rearrange("p a t -> p (a t)"), bank(7, T),
                               ACT.Copy).then_inc(aoT_ev, 1)
                for u in range(4):
                    act.wait_ge(as_ready, 4 * i + u + 1)
                    act.activation(probs[u], probs[u], ACT.Exp, bias=negmax[:, u:u + 1],
                                   accum_out=den[:, u:u + 1]).then_inc(ap_ready, 1)
                for u in (0, 2):
                    act.wait_ge(apt_done, 4 * i + u + 1)
                    act.activation(probsT[u], s_cols(u), ACT.Copy).then_inc(apt_act, 1)
            act.wait_ge(aoT_done, PAIRS + 1)
            act.activation(oAT[:, PAIRS, :], bank(7, T), ACT.Copy).then_inc(aoT_ev, 1)

            with act.Fori(0, RET_HEADS) as i:
                act.wait_ge(rqk_done, i + 1)
                act.activation(qkR[:, :, :].rearrange("p a t -> p (a t)"), bank(0), ACT.Copy).then_inc(rqk_ev, 1)
                act.wait_ge(roT_done, i + 1)
                act.activation(oRT[:, bass.ds(2 * i, 2), :].rearrange("p a t -> p (a t)"), bank(5),
                               ACT.Copy).then_inc(roT_ev, 1)
                act.wait_ge(rv_done, i + 1)
                act.activation(vR[:, :, :].rearrange("p a t -> p (a t)"), bank(1), ACT.Copy).then_inc(rv_ev, 1)
                act.wait_ge(rg_done, i + 1)
                act.activation(swish[:, :, :].rearrange("p a t -> p (a t)"), bank(2), ACT.Exp,
                               scale=-1.0).then_inc(rexp, 1)
            with act.Fori(0, GI) as i:
                for a in range(2):
                    act.wait_ge(g_done, 2 * i + a + 1)
                    act.wait_ge(g_ready, 2 * i + a + 1)
                    act.activation(eG[:, a, :, :].rearrange("p c t -> p (c t)"), bank(a), ACT.Exp,
                                   scale=-1.0).then_inc(g_exp, 1)

            act.wait_ge(roT_done, RET_HEADS + 1)
            act.activation(oRT[:, 2 * RET_HEADS:, :].rearrange("p a t -> p (a t)"), bank(5),
                           ACT.Copy).then_inc(roT_ev, 1)

            def squares(n):
                for t in range(TT):
                    act.wait_ge(sq_done, TT * n + t)
                    act.activation(junk[:, :], ps[:, 4 + 2 * t:6 + 2 * t, :].rearrange("p b n -> p (b n)"),
                                   ACT.Square, accum_out=ss[:, n, t:t + 1]).then_inc(sq_done, 1)

            act.wait_ge(wo_done, 2)
            squares(1)
            hT_copy(1)
            for t in range(TT):
                act.wait_ge(d_route, 1)
                act.activation(ra[:, t, 0:N_GROUPS], ra[:, t, 0:N_GROUPS], ACT.Exp,
                               accum_out=r1[:, 2, t:t + 1]).then_inc(gexp, 1)
            act.wait_ge(d_route, 2)
            act.activation(r1[:, 6, :], r1[:, 5, :], ACT.Exp).then_inc(e2exp, 1)

            act.wait_ge(sched_ready, 1)
            with act.Fori(0, NP) as p:
                R = act.value_load(sched[0:1, 0, bass.ds(p, 1)], min_val=1, max_val=ROUNDS)
                C = act.value_load(sched[0:1, 1, bass.ds(p, 1)], min_val=0, max_val=ROUNDS * NP)
                with act.Fori(0, R) as r:
                    n = C + r
                    act.wait_ge(gather_lo, n + 1)
                    act.activation(xg[:, 0:4, :].rearrange("p k s -> p (k s)"), bank(0), ACT.Copy).then_inc(xg_act, 1)
                    act.wait_ge(trY, 2 * n + 1)
                    act.activation(yS[:, 0:HALF], bank(3), ACT.Copy).then_inc(yS_act, 1)
                    for j in range(2):
                        act.wait_ge(gu_done[j], n + 1)
                        act.activation(sg[:, j, :], bank(2 + j, FT * SLOTS), ACT.Silu).then_inc(silu_done[j], 1)
                    for j in range(2):
                        act.wait_ge(down_done[j], n + 1)
                        act.activation(yT[:, :, j * SLOTS:(j + 1) * SLOTS],
                                       bank(j).rearrange("p (d s) -> p d s", s=SLOTS), ACT.Copy).then_inc(yT_ev, 1)
            CL = act.value_load(sched[0:1, 1, NP - 1:NP], min_val=0, max_val=ROUNDS * NP)
            RL = act.value_load(sched[0:1, 0, NP - 1:NP], min_val=1, max_val=ROUNDS)
            act.wait_ge(trY, 2 * (CL + RL) + 1)
            act.activation(yS[:, 0:HALF], bank(3), ACT.Copy).then_inc(yS_act, 1)
            act.wait_ge(scatter_done, 2 * (CL + RL) + 2)
            squares(2)

        @block.vector
        def _(dve):
            link, _n = chain(dve, dve_chain, 0)

            def mean_square(n):
                dve.wait_ge(sq_done, 2 * n + 2)
                dve.tensor_scalar(ms[:, n, :], ss[:, n, :], 1.0 / D, EPS, ALU.mult, ALU.add).then_inc(ms_done, 1)

            def permuted(ap):
                return ap.rearrange("q (p k) -> q k p", k=KT)

            dve.wait_ge(const_ready, 3)
            link(dve.tensor_copy(dist[:, :], dist_i[:, :]))
            for g, (window, dil) in enumerate(GROUPS):
                link(dve.tensor_single_scalar(resid_i[:, :], dist_i[:, :], dil - 1, ALU.bitwise_and))
                link(dve.tensor_copy(resid_f[:, :], resid_i[:, :]))
                link(dve.scalar_tensor_tensor(bias_t[:, g, :], resid_f[:, :], MASKED, dist[:, :], ALU.mult, ALU.add))
                for cmp, lim in ((ALU.is_gt, 0.0), (ALU.is_lt, float(-window))):
                    link(dve.tensor_single_scalar(resid_f[:, :], dist[:, :], lim, cmp))
                    link(dve.scalar_tensor_tensor(bias_t[:, g, :], resid_f[:, :], MASKED, bias_t[:, g, :],
                                                  ALU.mult, ALU.add))
            for j in range(2):
                link(dve.memset(slope[:, j:j + 1], 2.0 ** (-8.0 * (j + 1) / HEADS)))
            dve.memset(oA[:, :, :], 0.0).then_inc(ao_ev, 1)
            dve.memset(oR[:, :, :], 0.0).then_inc(r_out, 1)
            dve.sem_inc(g_ready, 2)

            mean_square(0)
            dve.wait_ge(s_g1, 16)
            dve.wait_ge(rstd_done, 1)
            for t in range(TT):
                dve.scalar_tensor_tensor(hn[:, t, :, :], permuted(xs[:, t, :]), rstd[:, 0, t:t + 1], permuted(g1[:, :]),
                                         ALU.mult, ALU.mult).then_inc(hn_done, 1)

            def hT_copy(n):
                dve.wait_ge(hT_psum, 2 * n + 2)
                dve.tensor_copy(hT[:, 4:8, :], ps[:, 2:4, :].rearrange("p b (k t) -> p (b k) t", k=2)).then_inc(hT_dve, 1)

            hT_copy(0)

            with dve.Fori(0, PAIRS) as i:
                dve.wait_ge(ak_done, i + 1)
                dve.tensor_copy(kT[:, :, :].rearrange("p g t -> p (g t)"),
                                ps[:, 2:4, :].rearrange("p b n -> p (b n)")[:, 0:NG * T]).then_inc(ak_ev, 1)
                for u in range(4):
                    span = T if u % 2 == 0 else P
                    dve.wait_ge(as_done, 4 * i + u + 1)
                    dve.scalar_tensor_tensor(probs[u].rearrange("p (g s) -> p g s", g=NG),
                                             bias_t[:, :, T - span:T], slope[:, u // 2:u // 2 + 1],
                                             s_cols(u).rearrange("p (g s) -> p g s", g=NG),
                                             ALU.mult, ALU.add).then_inc(as_chain, 1)
                    dve.wait_ge(as_chain, 4 * i + u + 1)
                    dve.tensor_reduce(negmax[:, u:u + 1], probs[u], AX_X, ALU.max, negate=True).then_inc(as_ready, 1)
                dve.tensor_scalar(slope[:, :], slope[:, :], 2.0 ** (-16.0 / HEADS), None, ALU.mult).then_inc(slope_chain, 1)
                dve.wait_ge(av_done, i + 1)
                dve.tensor_copy(vA[:, :, :, :].rearrange("p a g n -> p a (g n)"), ps[:, 0:2, 0:NG * P]).then_inc(av_ev, 1)
                for u in (1, 3):
                    dve.wait_ge(apt_done, 4 * i + u + 1)
                    dve.tensor_copy(probsT[u], s_cols(u)).then_inc(apt_dve, 1)
                dve.wait_ge(ap_ready, 4 * i + 4)
                dve.reciprocal(rden[:, :], den[:, :]).then_inc(ao_rden, 1)
                dve.wait_ge(ao_rden, i + 1)
                dve.wait_ge(ao_done, i + 1)
                for u in range(4):
                    j, t = u // 2, 1 - u % 2
                    ins = dve.tensor_scalar(oA[:, t, j * HEAD_DIM:(j + 1) * HEAD_DIM],
                                            ps[:, 6, t * P + j * HEAD_DIM:t * P + (j + 1) * HEAD_DIM],
                                            rden[:, u:u + 1], None, ALU.mult)
                ins.then_inc(ao_ev, 1)
                dve.wait_ge(slope_chain, i + 1)

            with dve.Fori(0, RET_HEADS) as i:
                rl, rn = chain(dve, r_chain, 2 * i)
                dve.wait_ge(decay_done, RET_HEADS)
                dve.wait_ge(rat_done, i + 1)
                dve.scalar_tensor_tensor(attR[:, :], bank(3, 3 * P), float(RK) ** -0.5,
                                         decay[:, bass.ds(i, 1), :].rearrange("p a n -> p (a n)"),
                                         ALU.mult, ALU.mult).then_inc(rat_ev, 1)
                sw = swish[:, :, :].rearrange("p a n -> p (a n)")
                dve.wait_ge(rexp, i + 1)
                rl(dve.tensor_scalar(sw, sw, 1.0, None, ALU.add))
                rl(dve.reciprocal(sw, sw))
                dve.wait_ge(ry_done, i + 1)
                for t in range(TT):
                    dve.bn_stats(stats[:, t, :], ps[:, 4, t * RV:(t + 1) * RV]).then_inc(r_stats, 1)
                dve.wait_ge(r_stats, TT * i + TT)
                dve.tensor_tensor(sw, sw, bank(2), ALU.mult).then_inc(r_swish, 1)
                for t in range(TT):
                    dve.bn_aggr(meanvar[:, t, :], stats[:, t, :]).then_inc(r_aggr, 1)
                dve.wait_ge(r_aggr, TT * i + TT)
                dve.tensor_scalar(meanvar[:, :, 1], meanvar[:, :, 1], EPS, None, ALU.add).then_inc(rvar, 1)
                assert rn[0] == 2
                dve.wait_ge(rrstd, i + 1)
                for t in range(TT):
                    ins = dve.tensor_scalar(oR[:, t, :], ps[:, 4, t * RV:(t + 1) * RV], meanvar[:, t, 0:1],
                                            rstdR[:, t:t + 1], ALU.subtract, ALU.mult)
                ins.then_inc(rpool, 1)
                dve.wait_ge(rpool, i + 1)
                dve.wait_ge(r_swish, i + 1)
                dve.tensor_tensor(oR[:, :, :], oR[:, :, :], swish[:, :, :], ALU.mult).then_inc(r_out, 1)

            with dve.Fori(0, GI) as i:
                for a, dst in ((0, gateA), (1, gateR)):
                    eg = eG[:, a, :, :].rearrange("p c t -> p (c t)")
                    dve.wait_ge(g_exp, 2 * i + a + 3)
                    dve.tensor_scalar(eg, eg, 1.0, None, ALU.add).then_inc(g_one, 1)
                    dve.wait_ge(g_one, 2 * i + a + 1)
                    dve.reciprocal(dst[:, bass.ds(2 * i, 2), :].rearrange("p c t -> p (c t)"), eg).then_inc(g_ready, 1)

            dve.wait_ge(g_ready, 2 * GI + 2)
            for b in range(KT // 2):
                dve.wait_ge(bA_done, b + 1)
                dve.tensor_tensor(merged[:, 2 * b:2 * b + 2, :], ps[:, 4 + b, :].rearrange("p (c t) -> p c t", c=2),
                                  gateA[:, 2 * b:2 * b + 2, :], ALU.mult).then_inc(bA_ev, 1)
            dve.wait_ge(bA_ev, KT // 2)
            for b in range(KT // 2):
                dve.wait_ge(bR_done, b + 1)
                dve.tensor_tensor(mtmp[:, :, :], ps[:, b, :].rearrange("p (c t) -> p c t", c=2),
                                  gateR[:, 2 * b:2 * b + 2, :], ALU.mult).then_inc(b_tmp, 1)
                dve.wait_ge(b_tmp, b + 1)
                dve.tensor_tensor(merged[:, 2 * b:2 * b + 2, :], merged[:, 2 * b:2 * b + 2, :], mtmp[:, :, :],
                                  ALU.add).then_inc(b_ready, 1)
                dve.wait_ge(b_ready, b + 1)

            def resid(t):
                return ps[:, 4 + 2 * t:6 + 2 * t, :].rearrange("p b n -> p (b n)")

            mean_square(1)
            dve.wait_ge(s_g2, 16)
            dve.wait_ge(rstd_done, 2)
            for t in range(TT):
                dve.scalar_tensor_tensor(hn[:, t, :, :], permuted(resid(t)), rstd[:, 1, t:t + 1], permuted(g2[:, :]),
                                         ALU.mult, ALU.mult).then_inc(hn_done, 1)
            hT_copy(1)

            dve.wait_ge(s_wr, 32)
            dve.wait_ge(logits_done, 1)
            dve.wait_ge(const_ready, 7)

            def per_row(k, n):
                return r1[:, k, :].unsqueeze(2).to_broadcast([P, TT, n])

            lp = ps[:, 0, 0:TT * 64].rearrange("p (a n) -> p a n", a=TT)[:, :, 0:NR]
            link(dve.tensor_tensor(lg[:, :, :], lp, br[:, :].unsqueeze(1).to_broadcast([P, TT, NR]), ALU.add))
            gl, el = lg[:, :, 0:N_GROUPS], lg[:, :, N_GROUPS:NR]
            rga, rgb = ra[:, :, 0:N_GROUPS], rb[:, :, 0:N_GROUPS]
            link(dve.tensor_reduce(r1[:, 0, :], gl, AX_X, ALU.max))
            link(dve.tensor_tensor(rb[:, :, 0:N_GROUPS], gl, per_row(0, N_GROUPS), ALU.is_equal))
            dve.tensor_tensor(rga, gl, per_row(0, N_GROUPS), ALU.subtract).then_inc(d_route, 1)

            def first_of(hits, n, k, dst):
                ids = rev_ids[:, 0:n].unsqueeze(1).to_broadcast([P, TT, n])
                link(dve.tensor_tensor(hits, hits, ids, ALU.mult))
                link(dve.tensor_reduce(r1[:, k, :], hits, AX_X, ALU.max))
                link(dve.tensor_tensor(dst, hits, per_row(k, n), ALU.is_equal))

            first_of(rgb, N_GROUPS, 1, rgb)
            link(dve.tensor_scalar(rgb, rgb, 1.0, -MASKED, ALU.subtract, ALU.mult))
            for t in range(TT):
                link(dve.tensor_tensor(el[:, t, :].rearrange("p (g n) -> p g n", g=N_GROUPS),
                                       el[:, t, :].rearrange("p (g n) -> p g n", g=N_GROUPS),
                                       rgb[:, t, :].unsqueeze(2).to_broadcast([P, N_GROUPS, PER_GROUP]), ALU.add))
            rbe = rb[:, :, N_GROUPS:NR]
            link(dve.tensor_reduce(r1[:, 3, :], el, AX_X, ALU.max))
            link(dve.tensor_tensor(rbe, el, per_row(3, E), ALU.is_equal))
            first_of(rbe, E, 7, oh1[:, :, :])
            link(dve.scalar_tensor_tensor(el, oh1[:, :, :], 2 * MASKED, el, ALU.mult, ALU.add))
            link(dve.tensor_reduce(r1[:, 4, :], el, AX_X, ALU.max))
            link(dve.tensor_tensor(rbe, el, per_row(4, E), ALU.is_equal))
            first_of(rbe, E, 8, oh2[:, :, :])
            dve.tensor_tensor(r1[:, 5, :], r1[:, 4, :], r1[:, 3, :], ALU.subtract).then_inc(d_route, 1)
            link(dve.tensor_tensor(sel[:, :, :], oh1[:, :, :], oh2[:, :, :], ALU.add))
            dve.tensor_tensor(sel_all[:, :], sel[:, 0, :], sel[:, 1, :], ALU.add).then_inc(sel_ready, 1)
            dve.wait_ge(gexp, TT)
            dve.wait_ge(e2exp, 1)
            link(dve.tensor_scalar(r1[:, 9, :], r1[:, 6, :], 1.0, None, ALU.add))
            link(dve.tensor_tensor(r1[:, 9, :], r1[:, 9, :], r1[:, 2, :], ALU.mult))
            link(dve.reciprocal(r1[:, 10, :], r1[:, 9, :]))
            link(dve.tensor_tensor(r1[:, 11, :], r1[:, 10, :], r1[:, 6, :], ALU.mult))
            link(dve.tensor_tensor(oh1[:, :, :], oh1[:, :, :], per_row(10, E), ALU.mult))
            link(dve.tensor_tensor(oh2[:, :, :], oh2[:, :, :], per_row(11, E), ALU.mult))
            link(dve.tensor_tensor(gate[:, :, :], oh1[:, :, :], oh2[:, :, :], ALU.add))
            dve.wait_ge(pos_done, 1)
            link(dve.tensor_copy(cnt[:, 0:2, :], ps[0:1, 2, 0:E].rearrange("p (n j) -> p j n", j=2)))
            link(dve.tensor_tensor(cnt[:, 2, :], cnt[:, 0, :], cnt[:, 1, :], ALU.max))
            link(dve.memset(sched_f[:, 0, :], 1.0))
            for r in range(1, ROUNDS):
                link(dve.scalar_tensor_tensor(sched_f[:, 0, :], cnt[:, 2, :], float(r * SLOTS), sched_f[:, 0, :],
                                              ALU.is_gt, ALU.add))
            link(dve.memset(sched_f[:, 1, 0:1], 0.0))
            link(dve.tensor_copy(sched_f[:, 1, 1:NP], sched_f[:, 0, 0:NP - 1]))
            a, b, step = 1, 2, 1
            while step < NP:
                link(dve.tensor_copy(sched_f[:, b, 0:step], sched_f[:, a, 0:step]))
                link(dve.tensor_tensor(sched_f[:, b, step:NP], sched_f[:, a, step:NP], sched_f[:, a, 0:NP - step], ALU.add))
                a, b, step = b, a, 2 * step
            link(dve.tensor_copy(sched[:, 0, :], sched_f[:, 0, :]))
            dve.tensor_copy(sched[:, 1, :], sched_f[:, a, :]).then_inc(sched_ready, 1)
            pp = ps[:, 1, 0:TT * E].rearrange("p (a n) -> p a n", a=TT)
            link(dve.scalar_tensor_tensor(pos[:, :, :], pp, 1.0, sel[:, :, :], ALU.add, ALU.mult))
            link(dve.tensor_scalar(pos[:, :, :], pos[:, :, :], 1.0, None, ALU.subtract))
            for j in range(2):
                dve.memset(hid[:, j, :], 0.0).then_inc(hid_ready[j], 1)
            dve.memset(gatedT[:, :], 0.0).then_inc(pgt_ev, 1)
            dve.memset(yT[:, :, :], 0.0).then_inc(yT_ev, 2)

            dve.wait_ge(sched_ready, 1)
            with dve.Fori(0, NP) as p:
                R = dve.value_load(sched[0:1, 0, bass.ds(p, 1)], min_val=1, max_val=ROUNDS)
                C = dve.value_load(sched[0:1, 1, bass.ds(p, 1)], min_val=0, max_val=ROUNDS * NP)
                with dve.Fori(0, R) as r:
                    n = C + r
                    ids = slot_ids[:, bass.ds(r * SLOTS, SLOTS)]

                    def mine(table, t, j):
                        return table[:, t, bass.ds(2 * p + j, 1)]

                    for t in range(TT):
                        for j in range(2):
                            ins = dve.tensor_scalar(onehot[:, t, j * SLOTS:(j + 1) * SLOTS], ids, mine(pos, t, j), None,
                                                    ALU.is_equal)
                    ins.then_inc(P_built, 1)
                    for t in range(TT):
                        for j in range(2):
                            ins = dve.tensor_scalar(gated[:, t, j * SLOTS:(j + 1) * SLOTS], ids, mine(pos, t, j),
                                                    mine(gate, t, j), ALU.is_equal, ALU.mult)
                    ins.then_inc(Pg_built, 1)
                    dve.wait_ge(gather_hi, n + 1)
                    dve.tensor_copy(xg[:, 4:8, :].rearrange("p k s -> p (k s)"), bank(1)).then_inc(xg_dve, 1)
                    dve.wait_ge(trY, 2 * n + 2)
                    dve.tensor_copy(yS[:, HALF:D], bank(3)).then_inc(yS_dve, 1)
                    for j in range(2):
                        dve.wait_ge(silu_done[j], n + 1)
                        dve.tensor_tensor(hid[:, j, :], sg[:, j, :], ps[:, 2 + j, FT * SLOTS:2 * FT * SLOTS],
                                          ALU.mult).then_inc(hid_ready[j], 1)
                    dve.wait_ge(pgt_done, n + 1)
                    dve.tensor_copy(gatedT[:, :], bank(1, T)).then_inc(pgt_ev, 1)
            CL = dve.value_load(sched[0:1, 1, NP - 1:NP], min_val=0, max_val=ROUNDS * NP)
            RL = dve.value_load(sched[0:1, 0, NP - 1:NP], min_val=1, max_val=ROUNDS)
            dve.wait_ge(trY, 2 * (CL + RL) + 2)
            dve.tensor_copy(yS[:, HALF:D], bank(3)).then_inc(yS_dve, 1)

            mean_square(2)
            dve.wait_ge(s_g3, 16)
            dve.wait_ge(rstd_done, 3)
            for t in range(TT):
                dve.scalar_tensor_tensor(res[:, t, :], resid(t), rstd[:, 2, t:t + 1], g3[:, :],
                                         ALU.mult, ALU.mult).then_inc(fin, 1)

        @block.tensor
        def _(pe):
            def mm(o, l, r, start, stop, shared=False):
                return pe.matmul(o, lhsT=l, rhs=r, start=start, stop=stop, skip_group_check=shared)

            def transpose_rows(n):
                pe.wait_ge(hn_done, 2 * n + 2)
                for k in range(KT):
                    for t in range(TT):
                        ins = pe.transpose(ps[:, k // 2, (k % 2) * T + t * P:(k % 2) * T + (t + 1) * P],
                                           hn[:, t, k, :], ident[:, :])
                    if k in (3, 7):
                        ins.then_inc(hT_psum, 1)
                pe.wait_ge(hT_act, n + 1)
                pe.wait_ge(hT_dve, n + 1)

            def columns(w, c0, n_tiles, b, off=0):
                for c in range(n_tiles):
                    o = off + c * T
                    for k in range(KT):
                        ins = mm(ps[:, b + o // 512, o % 512:o % 512 + T], w[:, k, c0 + c * P:c0 + (c + 1) * P],
                                 hT[:, k, :], k == 0, k == KT - 1)
                return ins

            def rows(w, n, outs):
                for t in range(TT):
                    for k in range(KT):
                        ins = mm(outs[t], hT[:, k, t * P:(t + 1) * P], w[:, k, 0:n], k == 0, k == KT - 1)
                return ins

            pe.wait_ge(const_ready, 1)
            transpose_rows(0)

            def transpose_attn(i):
                pe.wait_ge(ao_ev, i + 1)
                for t in range(TT):
                    ins = pe.transpose(ps[:, 7, t * P:(t + 1) * P], oA[:, t, :], ident[:, :])
                ins.then_inc(aoT_done, 1)

            with pe.Fori(0, PAIRS) as i:
                pe.wait_ge(s_w[0], 16 * (i + 1))
                columns(a_w[0], 0, NG, 0).then_inc(aq_done, 1)
                pe.wait_ge(s_w[1], 16 * (i + 1))
                columns(a_w[1], 0, NG, 2).then_inc(ak_done, 1)
                transpose_attn(i)
                pe.wait_ge(aq_ev, i + 1)
                pe.wait_ge(ak_ev, i + 1)
                for u in range(4):
                    j, t = u // 2, 1 - u % 2
                    h0, span = j * HEAD_DIM, (t + 1) * P
                    if u == 3:
                        pe.wait_ge(aoT_ev, i + 2)
                    for g in range(NG):
                        ins = mm(s_cols(u)[:, g * span:(g + 1) * span], qT[h0:h0 + HEAD_DIM, g, t * P:(t + 1) * P],
                                 kT[h0:h0 + HEAD_DIM, g, 0:span], True, True)
                    ins.then_inc(as_done, 1)
                pe.wait_ge(s_w[2], 16 * (i + 1))
                rows(a_w[2], NG * P, [bank(0, NG * P), bank(1, NG * P)]).then_inc(av_done, 1)
                for u in range(4):
                    pe.wait_ge(ap_ready, 4 * i + u + 1)
                    for c in range(UC[u % 2] // P):
                        ins = pe.transpose(s_cols(u)[:, c * P:(c + 1) * P], probs[u][:, c * P:(c + 1) * P], ident[:, :])
                    ins.then_inc(apt_done, 1)
                pe.wait_ge(av_ev, i + 1)
                pe.wait_ge(apt_dve, 2 * i + 1)
                for u in range(4):
                    j, t = u // 2, 1 - u % 2
                    if u % 2 == 0:
                        pe.wait_ge(apt_act, 2 * i + u // 2 + 1)
                    else:
                        pe.wait_ge(apt_dve, 2 * i + u // 2 + 1)
                    n_blocks = UC[u % 2] // P
                    for c in range(n_blocks):
                        g, s = c // (t + 1), c % (t + 1)
                        ins = mm(ps[:, 6, t * P + j * HEAD_DIM:t * P + (j + 1) * HEAD_DIM],
                                 probsT[u][:, c * P:(c + 1) * P], vA[:, s, g, j * HEAD_DIM:(j + 1) * HEAD_DIM],
                                 c == 0, c == n_blocks - 1)
                ins.then_inc(ao_done, 1)
            transpose_attn(PAIRS)

            def transpose_ret(i):
                pe.wait_ge(r_out, i + 1)
                pe.wait_ge(roT_ev, i + 1)
                for c in range(2):
                    for t in range(TT):
                        ins = pe.transpose(ps[:, 5, c * T + t * P:c * T + (t + 1) * P], oR[:, t, c * P:(c + 1) * P],
                                           ident[:, :])
                ins.then_inc(roT_done, 1)

            with pe.Fori(0, RET_HEADS) as i:
                pe.wait_ge(s_w[0], BASE_R + 32 + 32 * i)
                columns(r_w[0], 0, 2, 0).then_inc(rqk_done, 1)
                transpose_ret(i)
                pe.wait_ge(s_w[1], BASE_R + 16 + 16 * i)
                rows(r_w[1], RV, [ps[:, 2, t * RV:(t + 1) * RV] for t in range(TT)]).then_inc(rg_done, 1)
                pe.wait_ge(rqk_ev, i + 1)
                mm(ps[:, 3, 0:T], qkR[:, 1, 0:P], qkR[:, 0, :], True, True)
                mm(ps[:, 3, T:T + P], qkR[:, 1, P:T], qkR[:, 0, P:T], True, True).then_inc(rat_done, 1)
                pe.wait_ge(s_w[2], BASE_R + 16 + 16 * i)
                rows(r_w[2], RV, [ps[:, 1, t * RV:(t + 1) * RV] for t in range(TT)]).then_inc(rv_done, 1)
                pe.wait_ge(rat_ev, i + 1)
                pe.wait_ge(rv_ev, i + 1)
                mm(ps[:, 4, 0:RV], attR[:, 0:P], vR[:, 0, :], True, True)
                mm(ps[:, 4, RV:2 * RV], attR[:, P:2 * P], vR[:, 0, :], True, False)
                mm(ps[:, 4, RV:2 * RV], attR[:, 2 * P:3 * P], vR[:, 1, :], False, True).then_inc(ry_done, 1)

            with pe.Fori(0, GI) as i:
                for a in range(2):
                    pe.wait_ge(s_w[a], BASE_G[a] + 16 + 16 * i)
                    pe.wait_ge(g_exp, 2 * i + a + 1)
                    columns(r_w[a], 0, 2, a).then_inc(g_done, 1)
            transpose_ret(RET_HEADS)

            pe.wait_ge(s_w[2], W_ATTN)
            pe.wait_ge(aoT_ev, PAIRS + 2)
            pe.wait_ge(roT_ev, RET_HEADS + 2)
            for j in range(KT):
                for c in range(PAIRS):
                    ins = mm(ps[:, 4 + j // 2, (j % 2) * T:(j % 2 + 1) * T], half_w[2][:, c, j * P:(j + 1) * P],
                             oAT[:, c + 1, :], c == 0, c == PAIRS - 1)
                if j % 2 == 1:
                    ins.then_inc(bA_done, 1)
            for s in range(2):
                pe.wait_ge(s_w[s], W_RET[s])
            pe.wait_ge(g_exp, 2 * GI + 2)
            for j in range(KT):
                for c in range(2 * RET_HEADS):
                    ins = mm(ps[:, j // 2, (j % 2) * T:(j % 2 + 1) * T], half_w[c // 4][:, c % 4, j * P:(j + 1) * P],
                             oRT[:, c + 2, :], c == 0, c == 2 * RET_HEADS - 1)
                if j % 2 == 1:
                    ins.then_inc(bR_done, 1)

            pe.wait_ge(bA_ev, KT // 2)
            for t in range(TT):
                for h in range(2):
                    mm(ps[:, 4 + 2 * t + h, :], ident[:, :], xs[:, t, h * HALF:(h + 1) * HALF], True, False, True)
            for s, js in ((2, range(0, 4)), (0, range(4, 8))):
                pe.wait_ge(s_w[s], W_OUT[0] if s == 2 else W_OUT[1])
                pe.wait_ge(b_ready, js[-1] // 2 + 1)
                for j in js:
                    for t in range(TT):
                        for h in range(2):
                            ins = mm(ps[:, 4 + 2 * t + h, :], merged[:, j, t * P:(t + 1) * P],
                                     half_w[s][:, j % 4, h * HALF:(h + 1) * HALF], False, False, True)
                ins.then_inc(wo_done, 1)

            transpose_rows(1)
            pe.wait_ge(s_wr, 32)
            for t in range(TT):
                for k in range(KT):
                    ins = mm(ps[:, 0, t * 64:t * 64 + NR], hT[:, k, t * P:(t + 1) * P], wr[:, k, :], k == 0, k == KT - 1)
            ins.then_inc(logits_done, 1)
            pe.wait_ge(sel_ready, 1)
            pe.wait_ge(const_ready, 7)
            mm(ps[:, 1, 0:E], before[:, :], sel[:, 0, :], True, True)
            mm(ps[:, 1, E:2 * E], ones[:, :], sel[:, 0, :], True, False)
            mm(ps[:, 1, E:2 * E], before[:, :], sel[:, 1, :], False, True)
            mm(ps[0:1, 2, 0:E], ones[:, 0:1], sel_all[:, :], True, True).then_inc(pos_done, 1)

            def transpose_out(h):
                for d in range(4):
                    ins = pe.transpose(ps[:, 3, d * P:(d + 1) * P], yT[:, 4 * h + d, :], ident[:, :])
                ins.then_inc(trY, 1)

            def scatter(h):
                for t in range(TT):
                    ins = mm(ps[:, 4 + 2 * t + h, :], gatedT[:, t * P:(t + 1) * P], yS[:, h * HALF:(h + 1) * HALF],
                             False, False, True)
                ins.then_inc(scatter_done, 1)

            def gate_up(j):
                for half, s in enumerate((WG[j], WU[j])):
                    for f in range(FT):
                        o = half * FT * SLOTS + f * SLOTS
                        for k in range(KT):
                            ins = mm(ps[:, 2 + j, o:o + SLOTS], pair_w[s][:, k, f * P:(f + 1) * P],
                                     xg[:, k, j * SLOTS:(j + 1) * SLOTS], k == 0, k == KT - 1)
                ins.then_inc(gu_done[j], 1)

            def down(j):
                for d in range(KT):
                    for f in range(FT):
                        ins = mm(ps[:, j, d * SLOTS:(d + 1) * SLOTS], pair_w[WD[j]][:, f, d * P:(d + 1) * P],
                                 hid[:, j, f * SLOTS:(f + 1) * SLOTS], f == 0, f == FT - 1)
                ins.then_inc(down_done[j], 1)

            pe.wait_ge(sched_ready, 1)
            with pe.Fori(0, NP) as p:
                R = pe.value_load(sched[0:1, 0, bass.ds(p, 1)], min_val=1, max_val=ROUNDS)
                C = pe.value_load(sched[0:1, 1, bass.ds(p, 1)], min_val=0, max_val=ROUNDS * NP)
                with pe.Fori(0, R) as r:
                    n = C + r
                    pe.wait_ge(P_built, n + 1)
                    pe.wait_ge(yT_ev, 2 * n + 2)
                    for k in range(KT):
                        for t in range(TT):
                            ins = mm(ps[:, k // 4, (k % 4) * P:(k % 4 + 1) * P], hn[:, t, k, :], onehot[:, t, :],
                                     t == 0, t == TT - 1)
                        if k in (3, 7):
                            ins.then_inc(gather_lo if k == 3 else gather_hi, 1)
                    pe.wait_ge(hid_ready[1], n + 1)
                    transpose_out(0)
                    pe.wait_ge(xg_act, n + 1)
                    pe.wait_ge(xg_dve, n + 1)
                    pe.wait_ge(s_w[0], BASE_E[0] + 16 + 16 * p)
                    pe.wait_ge(s_w[1], BASE_E[1] + 16 + 16 * p)
                    gate_up(0)
                    pe.wait_ge(yS_act, n + 1)
                    transpose_out(1)
                    pe.wait_ge(pgt_ev, n + 1)
                    scatter(0)
                    pe.wait_ge(yS_dve, n + 1)
                    pe.wait_ge(s_w[2], BASE_E[2] + 16 + 16 * p)
                    pe.wait_ge(s_w[3], BASE_E[3] + 16 + 16 * p)
                    gate_up(1)
                    scatter(1)
                    pe.wait_ge(Pg_built, n + 1)
                    for t in range(TT):
                        ins = pe.transpose(ps[:, 1, t * P:(t + 1) * P], gated[:, t, :], ident[:, :])
                    ins.then_inc(pgt_done, 1)
                    pe.wait_ge(s_w[4], BASE_E[4] + 16 + 16 * p)
                    pe.wait_ge(hid_ready[0], n + 2)
                    down(0)
                    pe.wait_ge(s_w[5], BASE_E[5] + 16 + 16 * p)
                    pe.wait_ge(hid_ready[1], n + 2)
                    pe.wait_ge(pgt_ev, n + 2)
                    down(1)
            CL = pe.value_load(sched[0:1, 1, NP - 1:NP], min_val=0, max_val=ROUNDS * NP)
            RL = pe.value_load(sched[0:1, 0, NP - 1:NP], min_val=1, max_val=ROUNDS)
            n = CL + RL
            pe.wait_ge(yT_ev, 2 * n + 2)
            transpose_out(0)
            pe.wait_ge(yS_act, n + 1)
            transpose_out(1)
            scatter(0)
            pe.wait_ge(yS_dve, n + 1)
            scatter(1)


_OUT = (1, 256, 1024)


def kernel(x, g_mix, w_in, w_attn_branch, w_ret_branch, w_out, g_ffn, w_group_router, b_group_router,
           w_expert_router, b_expert_router, w_gate, w_up, w_down, g_final):
    import concourse.bacc as _bacc
    from concourse.bass_utils import run_bass_kernel_spmd as _run

    nc = _bacc.Bacc("TRN2", target_bir_lowering=False, num_devices=1)
    given = {
        "x": np.asarray(x)[0],
        "g_mix": np.asarray(g_mix)[0],
        "w_in": np.asarray(w_in)[0],
        "w_attn": np.asarray(w_attn_branch)[0],
        "w_ret": np.asarray(w_ret_branch)[0],
        "w_out": np.asarray(w_out)[0],
        "g_ffn": np.asarray(g_ffn)[0],
        "w_router": np.concatenate([np.asarray(w_group_router)[0], np.asarray(w_expert_router)[0]], axis=1),
        "b_router": np.concatenate([np.asarray(b_group_router)[0], np.asarray(b_expert_router)[0]]),
        "w_gate": np.asarray(w_gate)[0],
        "w_up": np.asarray(w_up)[0],
        "w_down": np.asarray(w_down)[0],
        "g_final": np.asarray(g_final),
    }
    arrays = {f"in_{n}": np.ascontiguousarray(a) for n, a in given.items()}
    aps = {n: nc.dram_tensor(f"in_{n}", arrays[f"in_{n}"].shape, mybir.dt.from_np(arrays[f"in_{n}"].dtype),
                             kind="ExternalInput").ap() for n in given}
    out = nc.dram_tensor("out_0", _OUT[1:], F32, kind="ExternalOutput").ap()
    hybrid_block(nc, out=out, **aps)
    r = _run(nc, [arrays], core_ids=[0])
    return r.results[0]["out_0"].reshape(_OUT)
```

```python
from contextlib import ExitStack

import numpy as np

import concourse.bass as bass
from concourse import mybir

ALU = mybir.AluOpType
ACT = mybir.ActivationFunctionType
AX_X = mybir.AxisListType.X
F32 = mybir.dt.float32
F32R = mybir.dt.float32r
I32 = mybir.dt.int32

P = 128
GROUPS = ((128, 1), (512, 4), (2048, 16))
HEADS = 8
HEAD_DIM = 64
RET_HEADS = 4
N_GROUPS = 4
PER_GROUP = 8
EPS = 1e-6
SLOTS = 64
MASKED = -1e30
RING = 6


def chain(eng, sem, base):
    count = [0]

    def link(ins):
        count[0] += 1
        ins.then_inc(sem, 1)
        eng.wait_ge(sem, base + count[0])

    return link, count


def hybrid_block(nc, x, g_mix, w_in, w_attn, w_ret, w_out, g_ffn, w_router, b_router,
                 w_gate, w_up, w_down, g_final, out):
    T, D = x.shape
    TT = T // P
    KT = D // P
    NG = len(GROUPS)
    AW = HEADS * HEAD_DIM
    RK = D // 8
    RV = 2 * RK
    E, _, FF = w_gate.shape
    FT = FF // P
    NP = E // 2
    PAIRS = HEADS // 2
    NR = N_GROUPS + E
    ROUNDS = T // SLOTS
    CH = 4
    HALF = D // 2
    assert TT == 2 and KT == 8 and RK == P and HALF == 512 and FT * P == 512 and E == N_GROUPS * PER_GROUP

    COL_Q, COL_K, COL_V = 0, NG * AW, 2 * NG * AW
    COL_RQ = 3 * NG * AW
    COL_RK = COL_RQ + RET_HEADS * RK
    COL_RV = COL_RK + RET_HEADS * RK
    COL_RG = COL_RV + RET_HEADS * RV
    COL_GA = COL_RG + RET_HEADS * RV
    COL_GR = COL_GA + D
    w_in_v = w_in.rearrange("(p k) n -> p k n", k=KT)
    wattn_v = w_attn.rearrange("(c p) n -> p c n", p=P)
    wret_v = w_ret.rearrange("(c p) n -> p c n", p=P)
    wout_v = w_out.rearrange("(c p) n -> p c n", p=P)
    wg_v = w_gate.rearrange("e (p k) f -> e p (k f)", k=KT)
    wu_v = w_up.rearrange("e (p k) f -> e p (k f)", k=KT)
    wd_v = w_down.rearrange("e (c p) d -> e p c d", p=P)
    attn_v = [w_in_v[:, :, c:c + NG * AW].rearrange("p k (g n) -> p k g n", g=NG) for c in (COL_Q, COL_K, COL_V)]
    qk_v = w_in_v[:, :, COL_RQ:COL_RV].rearrange("p k (h n) -> p k h n", h=2)
    gates_v = w_in_v[:, :, COL_GA:COL_GA + 2 * D].rearrange("p k (h n) -> p k h n", h=2)
    x_v = x.rearrange("(a p) d -> p a d", p=P)
    out_v = out.rearrange("(a p) d -> p a d", p=P)

    with ExitStack() as ctx:
        def sb(name, shape, dt=F32):
            return ctx.enter_context(nc.sbuf_tensor(name, shape, dt))

        def sem(name):
            return ctx.enter_context(nc.semaphore(name))

        ps = ctx.enter_context(nc.psum_tensor("ps", [P, 8, 512], F32))

        RAW = 1024
        ring_at = -(-nc.sbuf_base // 32) * 32
        ring = sb("ring", [P, 6, 4096])
        split = nc.alloc_sbuf_tensor_at("split", [P, CH, 2, RAW], F32R, offset=ring_at + 4096 * 4)
        xs = sb("xs", [P, TT, D])
        hn = sb("hn", [P, TT, KT, P])
        hT = sb("hT", [P, 2, KT, T], F32R)
        gain = sb("gain", [P, D])
        ident = sb("ident", [P, P])
        before = sb("before", [P, P])
        ones = sb("ones", [P, P])
        bias_t = sb("bias_t", [P, NG, T])
        slope = sb("slope", [P, 2])
        decay = sb("decay", [P, RET_HEADS, T])
        age = sb("age", [P, T])
        half_neg = sb("half_neg", [P, 2])
        slot_ids = sb("slot_ids", [P, ROUNDS * SLOTS])
        rev_ids = sb("rev_ids", [P, NR])
        ss = sb("ss", [P, 3, TT])
        ms = sb("ms", [P, 3, TT])
        rstd = sb("rstd", [P, 3, TT])

        mid = sb("mid", [P, 2 * KT * T])
        qT = mid[:, 0:NG * T].rearrange("p (g t) -> p g t", g=NG)
        kT = mid[:, NG * T:2 * NG * T].rearrange("p (g t) -> p g t", g=NG)
        vA = mid[:, 2 * NG * T:2 * NG * T + TT * NG * P].rearrange("p (a g n) -> p a g n", a=TT, g=NG)
        gateA = mid[:, 0:KT * T].rearrange("p (k t) -> p k t", k=KT)
        gateR = mid[:, KT * T:2 * KT * T].rearrange("p (k t) -> p k t", k=KT)
        h2T = mid[:, 0:KT * T].rearrange("p (k t) -> p k t", k=KT)

        UC = [NG * T, NG * P]
        work = sb("work", [P, 4 * (UC[0] + UC[1])])

        def carve(at):
            def take(n):
                at[0] += n
                return work[:, at[0] - n:at[0]]
            return take

        take = carve([0])
        probs = [take(UC[u % 2]) for u in range(4)]
        probsT = [take(UC[u % 2]) for u in range(4)]
        take = carve([0])
        junk = take(D)
        dist_i = take(T).bitcast(I32)
        resid_i = take(T).bitcast(I32)
        resid_f = take(T)
        dist = take(T)
        take = carve([0])
        qkR = take(2 * T).rearrange("p (a t) -> p a t", a=2)
        vR = take(TT * RV).rearrange("p (a n) -> p a n", a=TT)
        attR = take(3 * P)
        swish = take(TT * RV).rearrange("p (a n) -> p a n", a=TT)
        take = carve([3072])
        oR = take(TT * RV).rearrange("p (a n) -> p a n", a=TT)
        take = carve([0])
        merged = take(KT * T).rearrange("p (k t) -> p k t", k=KT)
        mtmp = take(2 * T).rearrange("p (k t) -> p k t", k=2)
        take = carve([0])
        xg = take(KT * P).rearrange("p (k s) -> p k s", k=KT)
        sg = take(FF)
        hid = take(FF)
        hidT = take(FT * P).rearrange("p (f s) -> p f s", f=FT)
        yS = take(D)
        onehot = take(TT * P).rearrange("p (a s) -> p a s", a=TT)
        gated = take(TT * P).rearrange("p (a s) -> p a s", a=TT)

        negmax = sb("negmax", [P, 4])
        den = sb("den", [P, 4])
        rden = sb("rden", [P, 4])
        oA = sb("oA", [P, TT, P])
        oAT = sb("oAT", [P, 2, PAIRS, T], F32R)
        oRT = sb("oRT", [P, 2, 2 * RET_HEADS, T], F32R)
        stats = sb("stats", [P, TT, 6])
        meanvar = sb("meanvar", [P, TT, 2])
        rstdR = sb("rstdR", [P, TT])
        gap = sb("gap", [P, 2])

        wr = sb("wr", [P, KT, NR])
        br = sb("br", [P, NR])
        lg = sb("lg", [P, TT, NR])
        ra = sb("ra", [P, TT, NR])
        rb = sb("rb", [P, TT, NR])
        r1 = sb("r1", [P, 12, TT])
        oh1 = sb("oh1", [P, TT, E])
        oh2 = sb("oh2", [P, TT, E])
        gate = sb("gate", [P, TT, E])
        sel = sb("sel", [P, TT, E])
        sel_all = sb("sel_all", [P, E])
        pos = sb("pos", [P, TT, E])
        cnt = sb("cnt", [1, 4, NP])
        sched_f = sb("sched_f", [1, 3, NP])
        sched = sb("sched", [1, 2, NP], I32)
        gatedT = sb("gatedT", [P, T])
        res = xs

        s_x = [sem(f"s_x{t}") for t in range(TT)]
        s_gain = sem("s_gain")
        s_wr = sem("s_wr")
        raw_loaded = [sem(f"raw_loaded{s}") for s in range(CH)]
        hi_ready, lo_ready, chunk_used = sem("hi_ready"), sem("lo_ready"), sem("chunk_used")
        s_e = [sem(f"s_e{i}") for i in range(6)]
        s_out = sem("s_out")
        const_ready = sem("const_ready")
        pool_chain = sem("pool_chain")
        dve_chain = sem("dve_chain")
        sq_done = sem("sq_done")
        ms_done = sem("ms_done")
        rstd_done = sem("rstd_done")
        hn_done = sem("hn_done")
        hT_psum = sem("hT_psum")
        hT_act = sem("hT_act")
        hT_dve = sem("hT_dve")
        age_done = sem("age_done")
        decay_done = sem("decay_done")

        aq_ev, ak_ev, av_ev = sem("aq_ev"), sem("ak_ev"), sem("av_ev")
        as_done, as_chain, as_ready = sem("as_done"), sem("as_chain"), sem("as_ready")
        slope_chain = sem("slope_chain")
        ap_ready = sem("ap_ready")
        apt_done, apt_act, apt_dve = sem("apt_done"), sem("apt_act"), sem("apt_dve")
        ao_done, ao_rden, ao_ev = sem("ao_done"), sem("ao_rden"), sem("ao_ev")
        aoT_done, aoT_hi, aoT_lo = sem("aoT_done"), sem("aoT_hi"), sem("aoT_lo")

        rqk_ev, rv_ev = sem("rqk_ev"), sem("rv_ev")
        rat_done, rat_ev = sem("rat_done"), sem("rat_ev")
        ry_done, r_stats, r_gap = sem("ry_done"), sem("r_stats"), sem("r_gap")
        r_aggr, rvar = sem("r_aggr"), sem("rvar")
        rrstd, r_norm, r_swish, r_out = sem("rrstd"), sem("r_norm"), sem("r_swish"), sem("r_out")
        roT_done, roT_hi, roT_lo = sem("roT_done"), sem("roT_hi"), sem("roT_lo")

        g_ready = sem("g_ready")
        bA_done, bR_done, bA_ev, b_tmp, b_sum = (sem("bA_done"), sem("bR_done"), sem("bA_ev"),
                                                 sem("b_tmp"), sem("b_sum"))
        b_hi, b_ready = sem("b_hi"), sem("b_ready")
        logits_done, gexp, e2exp = sem("logits_done"), sem("gexp"), sem("e2exp")
        d_route = sem("d_route")
        sel_ready, pos_done, sched_ready = sem("sel_ready"), sem("pos_done"), sem("sched_ready")

        P_built, Pg_built = sem("P_built"), sem("Pg_built")
        gather_lo, gather_hi = sem("gather_lo"), sem("gather_hi")
        xg_act, xg_dve = sem("xg_act"), sem("xg_dve")
        gate_done, up_done, silu_done, hid_ready = sem("gate_done"), sem("up_done"), sem("silu_done"), sem("hid_ready")
        hidT_done, hidT_ev = sem("hidT_done"), sem("hidT_ev")
        pgt_done, pgt_ev = sem("pgt_done"), sem("pgt_ev")
        down_done = [sem(f"down_done{h}") for h in range(2)]
        yS_ev = [sem(f"yS_ev{h}") for h in range(2)]
        scatter_done = sem("scatter_done")
        fin = sem("fin")

        GI = D // 256
        Q_RET = 3 * PAIRS
        Q_GATE = Q_RET + 3 * RET_HEADS
        Q_ATTN = Q_GATE + GI
        Q_WRET = Q_ATTN + PAIRS // CH
        Q_OUT = Q_WRET + 2 * RET_HEADS // CH
        QUADS = Q_OUT + KT // CH
        W_A, W_R, W_G, W_B = 2 * NG * P, 2 * RV, 2 * 512, D

        def raw(s, n):
            return ring[:, 0, s * RAW:s * RAW + n]

        def parts(s, n, steps):
            return [split[:, s, a, 0:n].rearrange("p (k n) -> p k n", k=steps) for a in range(2)]

        pair_gate = [ring[:, s, :].rearrange("p (k n) -> p k n", k=KT) for s in (0, 1)]
        pair_up = [ring[:, s, :].rearrange("p (k n) -> p k n", k=KT) for s in (2, 3)]
        pair_down = [ring[:, s, :].rearrange("p (c n) -> p c n", c=FT) for s in (4, 5)]

        def bank(b, n=512):
            return ps[:, b, 0:n]

        def banks(b, n=1024):
            return ps[:, b:b + 2, :].rearrange("p b n -> p (b n)")[:, 0:n]

        def s_cols(u):
            return (banks(4, UC[0]), bank(6, UC[1]), banks(2, UC[0]), bank(7, UC[1]))[u]

        block = ctx.enter_context(nc.Block())

        @block.sync
        def _(sp):
            for t in range(TT):
                sp.dma_start(xs[:, t, :], x_v[:, t, :]).then_inc(s_x[t], 16)
            sp.dma_start(gain[:, :], g_mix.partition_broadcast(P)).then_inc(s_gain, 16)

            def load_quad(Q, piece):
                for s in range(CH):
                    if not isinstance(Q, int) or Q > 0:
                        sp.wait_ge(lo_ready, CH * Q + s + 1 - CH)
                    for m in range(2):
                        sp.dma_start(*piece(s, m)).then_inc(raw_loaded[s], 16)

            def columns_of(view, n_parts, width, i):
                def piece(s, m):
                    dst = raw(s, 2 * n_parts * width).rearrange("p (k g n) -> p k g n", k=2, g=n_parts)
                    return dst[:, m], view[:, 2 * s + m, :, bass.ds(i * width, width)]
                return piece

            def plain_columns(col, width, i):
                def piece(s, m):
                    dst = raw(s, 2 * width).rearrange("p (k n) -> p k n", k=2)
                    return dst[:, m], w_in_v[:, 2 * s + m, bass.ds(col + i * width, width)]
                return piece

            def full_rows(view, c):
                def piece(s, m):
                    return raw(s, D)[:, m * HALF:(m + 1) * HALF], view[:, c + s, m * HALF:(m + 1) * HALF]
                return piece

            def load_pair(i):
                for m in range(3):
                    load_quad(3 * i + m, columns_of(attn_v[m], NG, P, i))

            load_pair(0)
            with sp.Fori(1, PAIRS) as i:
                load_pair(i)
            sp.dma_start(ring[:, 3, :], wu_v[1]).then_inc(s_e[3], 16)
            with sp.Fori(0, RET_HEADS) as i:
                load_quad(Q_RET + 3 * i, columns_of(qk_v, 2, RK, i))
                load_quad(Q_RET + 1 + 3 * i, plain_columns(COL_RG, RV, i))
                load_quad(Q_RET + 2 + 3 * i, plain_columns(COL_RV, RV, i))
            sp.dma_start(pair_down[0], wd_v[0]).then_inc(s_e[4], 16)
            with sp.Fori(0, GI) as i:
                load_quad(Q_GATE + i, columns_of(gates_v, 2, 256, i))
            sp.dma_start(pair_down[1], wd_v[1]).then_inc(s_e[5], 16)
            for Q, view, c in ((Q_ATTN, wattn_v, 0), (Q_WRET, wret_v, 0), (Q_WRET + 1, wret_v, CH),
                               (Q_OUT, wout_v, 0), (Q_OUT + 1, wout_v, CH)):
                load_quad(Q, full_rows(view, c))
            sp.wait_ge(hn_done, TT)
            sp.dma_start(gain[:, :], g_ffn.partition_broadcast(P)).then_inc(s_gain, 16)
            sp.wait_ge(lo_ready, CH * QUADS)
            sp.dma_start(ring[:, 0, :], wg_v[0]).then_inc(s_e[0], 16)
            sp.wait_ge(chunk_used, CH * QUADS)
            sp.dma_start(ring[:, 1, :], wg_v[1]).then_inc(s_e[1], 16)
            sp.dma_start(ring[:, 2, :], wu_v[0]).then_inc(s_e[2], 16)
            sp.wait_ge(hn_done, 2 * TT)
            sp.dma_start(gain[:, :], g_final.partition_broadcast(P)).then_inc(s_gain, 16)

            sp.wait_ge(sched_ready, 1)
            with sp.Fori(1, NP) as p:
                C = sp.value_load(sched[0:1, 1, bass.ds(p, 1)], min_val=1, max_val=ROUNDS * NP)
                for slot, view, done in ((0, wg_v, gate_done), (2, wu_v, up_done), (4, wd_v, down_done[1])):
                    sp.wait_ge(done, C)
                    for j in range(2):
                        src = view[bass.ds(2 * p + j, 1)]
                        if slot == 4:
                            sp.dma_start(pair_down[j], src.rearrange("e p c n -> (e p) c n")).then_inc(s_e[4 + j], 16)
                        else:
                            sp.dma_start(ring[:, slot + j, :], src.rearrange("e p n -> (e p) n")).then_inc(s_e[slot + j], 16)

            for t in range(TT):
                sp.wait_ge(fin, t + 1)
                sp.dma_start(out_v[:, t, :], res[:, t, :]).then_inc(s_out, 16)
            sp.wait_ge(s_out, 16 * TT)

        @block.gpsimd
        def _(pool):
            link, _n = chain(pool, pool_chain, 0)
            link(pool.memset(ident[:, :], 0.0))
            pool.affine_select(out=ident[:, :], in_=ident[:, :], compare_op=ALU.not_equal, fill=1.0, base=0,
                               pattern=[[-1, P]], channel_multiplier=1).then_inc(const_ready, 1)
            pool.memset(half_neg[:, :], -0.5).then_inc(const_ready, 1)
            pool.wait_ge(sq_done, TT)
            pool.iota(dist_i[:, :], pattern=[[1, T]], base=-P, channel_multiplier=-1).then_inc(const_ready, 1)

            def inv_root(n):
                pool.wait_ge(ms_done, n + 1)
                pool.tensor_tensor(out=rstd[:, n, :], in0=ms[:, n, :], in1=half_neg[:, 0:TT],
                                   op=ALU.pow).then_inc(rstd_done, 1)

            pool.wait_ge(const_ready, 3)
            inv_root(0)
            link(pool.iota(age[:, :], pattern=[[1, T]], base=0, channel_multiplier=-1,
                           allow_small_or_imprecise_dtypes=True))
            pool.affine_select(out=age[:, 0:P], in_=age[:, 0:P], compare_op=ALU.is_ge, fill=-MASKED, base=0,
                               pattern=[[1, P]], channel_multiplier=-1).then_inc(age_done, 1)
            link(pool.memset(before[:, :], 1.0))
            pool.affine_select(out=before[:, :], in_=before[:, :], compare_op=ALU.is_gt, fill=0.0, base=0,
                               pattern=[[1, P]], channel_multiplier=-1).then_inc(const_ready, 1)
            pool.memset(ones[:, :], 1.0).then_inc(const_ready, 1)
            pool.iota(slot_ids[:, :], pattern=[[1, ROUNDS * SLOTS]], base=0, channel_multiplier=0,
                      allow_small_or_imprecise_dtypes=True).then_inc(const_ready, 1)
            pool.iota(rev_ids[:, :], pattern=[[-1, NR]], base=NR, channel_multiplier=0,
                      allow_small_or_imprecise_dtypes=True).then_inc(const_ready, 1)
            with pool.Fori(0, RET_HEADS) as i:
                pool.wait_ge(rvar, i + 1)
                pool.tensor_tensor(out=rstdR[:, :], in0=meanvar[:, :, 1], in1=half_neg[:, 0:TT],
                                   op=ALU.pow).then_inc(rrstd, 1)
            inv_root(1)
            inv_root(2)

        @block.scalar
        def _(act):
            act.dma_start(wr[:, :, :], w_router.rearrange("(p k) n -> p k n", k=KT)).then_inc(s_wr, 16)
            act.dma_start(br[:, :], b_router.partition_broadcast(P)).then_inc(s_wr, 16)

            def high(Q, s, n):
                act.wait_ge(raw_loaded[s], 32 * Q + 32)
                if not isinstance(Q, int) or Q > 0:
                    act.wait_ge(chunk_used, CH * Q + s + 1 - CH)
                act.activation(split[:, s, 0, 0:n], raw(s, n), ACT.Copy).then_inc(hi_ready, 1)

            for t in range(TT):
                act.wait_ge(s_x[t], 16)
                if t > 0:
                    act.wait_ge(sq_done, t)
                act.activation(junk, xs[:, t, :], ACT.Square, accum_out=ss[:, 0, t:t + 1]).then_inc(sq_done, 1)
            for s in range(CH):
                high(0, s, W_A)
            for b in (0, 2):
                act.wait_ge(hT_psum, b // 2 + 1)
                act.activation(hT[:, 0, 2 * b:2 * b + 4, :].rearrange("p k t -> p (k t)"), banks(b),
                               ACT.Copy).then_inc(hT_act, 1)
            act.wait_ge(age_done, 1)
            for h in range(RET_HEADS):
                act.activation(decay[:, h, :], age[:, :], ACT.Exp,
                               scale=float(np.log1p(-2.0 ** (-5.0 - h)))).then_inc(decay_done, 1)

            def attention(i, n_next):
                for s in range(CH):
                    high(3 * i + 1, s, W_A)
                act.wait_ge(chunk_used, CH * (3 * i + 1))
                act.activation(qT.rearrange("p g t -> p (g t)"), banks(0, NG * T), ACT.Copy,
                               scale=float(HEAD_DIM) ** -0.5).then_inc(aq_ev, 1)
                act.wait_ge(aoT_done, i + 1)
                act.activation(oAT[:, 0, bass.ds(i, 1), :].rearrange("p a t -> p (a t)"), bank(7, T),
                               ACT.Copy).then_inc(aoT_hi, 1)
                for s in range(CH):
                    high(3 * i + 2, s, W_A)
                for u in range(4):
                    act.wait_ge(as_ready, 4 * i + u + 1)
                    act.activation(probs[u], probs[u], ACT.Exp, bias=negmax[:, u:u + 1],
                                   accum_out=den[:, u:u + 1]).then_inc(ap_ready, 1)
                for s in range(CH):
                    high(3 * i + 3, s, n_next)
                for u in (0, 2):
                    act.wait_ge(apt_done, 4 * i + u + 1)
                    act.activation(probsT[u], s_cols(u), ACT.Copy).then_inc(apt_act, 1)

            with act.Fori(0, PAIRS - 1) as i:
                attention(i, W_A)
            attention(PAIRS - 1, W_R)
            act.wait_ge(aoT_done, PAIRS + 1)
            act.activation(oAT[:, 0, 0, :], bank(7, T), ACT.Copy).then_inc(aoT_hi, 1)

            def retention(i, n_next):
                for s in range(CH):
                    high(Q_RET + 1 + 3 * i, s, W_R)
                act.wait_ge(chunk_used, CH * (Q_RET + 1 + 3 * i))
                act.activation(qkR.rearrange("p a t -> p (a t)"), bank(0), ACT.Copy).then_inc(rqk_ev, 1)
                act.wait_ge(roT_done, i + 1)
                act.activation(oRT[:, 0, bass.ds(2 * i, 2), :].rearrange("p a t -> p (a t)"), bank(5),
                               ACT.Copy).then_inc(roT_hi, 1)
                for s in range(CH):
                    high(Q_RET + 2 + 3 * i, s, W_R)
                act.wait_ge(chunk_used, CH * (Q_RET + 2 + 3 * i))
                act.activation(swish.rearrange("p a t -> p (a t)"), bank(2), ACT.Silu).then_inc(r_swish, 1)
                for s in range(CH):
                    if s == CH - 1:
                        act.wait_ge(chunk_used, CH * (Q_RET + 3 + 3 * i))
                        act.activation(vR.rearrange("p a t -> p (a t)"), bank(1), ACT.Copy).then_inc(rv_ev, 1)
                    high(Q_RET + 3 + 3 * i, s, n_next)

            with act.Fori(0, RET_HEADS - 1) as i:
                retention(i, W_R)
            retention(RET_HEADS - 1, W_G)

            with act.Fori(0, GI // 2) as i:
                for m in range(2):
                    for s in range(CH):
                        high(Q_GATE + 1 + m + 2 * i, s, W_G)
                    act.wait_ge(chunk_used, CH * (Q_GATE + m + 1 + 2 * i))
                    for a, dst in ((0, gateA), (1, gateR)):
                        act.activation(dst[:, bass.ds(4 * i + 2 * m, 2), :].rearrange("p c t -> p (c t)"),
                                       bank(2 * m + a), ACT.Sigmoid).then_inc(g_ready, 1)
            act.wait_ge(roT_done, RET_HEADS + 1)
            act.activation(oRT[:, 0, 0:2, :].rearrange("p a t -> p (a t)"), bank(5), ACT.Copy).then_inc(roT_hi, 1)
            for Q in (Q_WRET, Q_WRET + 1, Q_OUT):
                for s in range(CH):
                    high(Q, s, W_B)
            for b in range(KT // 2):
                act.wait_ge(b_sum, b + 1)
                act.activation(hT[:, 0, 2 * b:2 * b + 2, :], merged[:, 2 * b:2 * b + 2, :], ACT.Copy).then_inc(b_hi, 1)
            for s in range(CH):
                high(Q_OUT + 1, s, W_B)

            def squares(n):
                for t in range(TT):
                    act.wait_ge(sq_done, TT * n + t)
                    act.activation(junk, banks(4 + 2 * t), ACT.Square, accum_out=ss[:, n, t:t + 1]).then_inc(sq_done, 1)

            act.wait_ge(chunk_used, CH * QUADS)
            squares(1)
            act.wait_ge(hT_psum, 3)
            act.activation(h2T[:, 0:4, :].rearrange("p k t -> p (k t)"), banks(0), ACT.Copy).then_inc(hT_act, 1)
            for t in range(TT):
                act.wait_ge(d_route, 1)
                act.activation(ra[:, t, 0:N_GROUPS], ra[:, t, 0:N_GROUPS], ACT.Exp,
                               accum_out=r1[:, 2, t:t + 1]).then_inc(gexp, 1)
            act.wait_ge(d_route, 2)
            act.activation(r1[:, 6, :], r1[:, 5, :], ACT.Exp).then_inc(e2exp, 1)

            act.wait_ge(sched_ready, 1)
            with act.Fori(0, NP) as p:
                R = act.value_load(sched[0:1, 0, bass.ds(p, 1)], min_val=1, max_val=ROUNDS)
                C = act.value_load(sched[0:1, 1, bass.ds(p, 1)], min_val=0, max_val=ROUNDS * NP)
                with act.Fori(0, R) as r:
                    n = C + r
                    act.wait_ge(gather_lo, n + 1)
                    act.activation(xg[:, 0:4, :].rearrange("p k s -> p (k s)"), bank(0), ACT.Copy).then_inc(xg_act, 1)
                    act.wait_ge(gate_done, n + 1)
                    act.activation(sg, bank(2), ACT.Silu).then_inc(silu_done, 1)
                    act.wait_ge(hidT_done, n + 1)
                    act.activation(hidT.rearrange("p f s -> p (f s)"), bank(0), ACT.Copy).then_inc(hidT_ev, 1)
                    for h in range(2):
                        act.wait_ge(down_done[h], n + 1)
                        act.activation(yS[:, h * HALF:(h + 1) * HALF], bank(2 + h), ACT.Copy).then_inc(yS_ev[h], 1)
            CL = act.value_load(sched[0:1, 1, NP - 1:NP], min_val=0, max_val=ROUNDS * NP)
            RL = act.value_load(sched[0:1, 0, NP - 1:NP], min_val=1, max_val=ROUNDS)
            act.wait_ge(scatter_done, 2 * (CL + RL) + 2)
            squares(2)

        @block.vector
        def _(dve):
            link, _n = chain(dve, dve_chain, 0)

            def low(Q, s, n):
                dve.wait_ge(hi_ready, CH * Q + s + 1)
                dve.tensor_tensor(split[:, s, 1, 0:n], raw(s, n), split[:, s, 0, 0:n].bitcast(F32),
                                  ALU.subtract).then_inc(lo_ready, 1)

            def mean_square(n):
                dve.wait_ge(sq_done, 2 * n + 2)
                dve.tensor_scalar(ms[:, n, :], ss[:, n, :], 1.0 / D, EPS, ALU.mult, ALU.add).then_inc(ms_done, 1)

            def permuted(ap):
                return ap.rearrange("q (p k) -> q k p", k=KT)

            for j in range(2):
                link(dve.memset(slope[:, j:j + 1], 2.0 ** (-8.0 * (j + 1) / HEADS)))
            dve.memset(oA[:, :, :], 0.0).then_inc(ao_ev, 1)
            dve.sem_inc(aoT_lo, 1)
            dve.sem_inc(roT_lo, 1)

            mean_square(0)
            for s in range(CH):
                low(0, s, W_A)
            dve.wait_ge(s_gain, 16)
            dve.wait_ge(rstd_done, 1)
            for t in range(TT):
                dve.scalar_tensor_tensor(hn[:, t, :, :], permuted(xs[:, t, :]), rstd[:, 0, t:t + 1], permuted(gain[:, :]),
                                         ALU.mult, ALU.mult).then_inc(hn_done, 1)
            for b in (0, 2):
                dve.wait_ge(hT_act, b // 2 + 1)
                dve.tensor_tensor(hT[:, 1, 2 * b:2 * b + 4, :].rearrange("p k t -> p (k t)"), banks(b),
                                  hT[:, 0, 2 * b:2 * b + 4, :].bitcast(F32).rearrange("p k t -> p (k t)"),
                                  ALU.subtract).then_inc(hT_dve, 1)

            dve.wait_ge(const_ready, 3)
            link(dve.tensor_copy(dist, dist_i))
            for g, (window, dil) in enumerate(GROUPS):
                link(dve.tensor_single_scalar(resid_i, dist_i, dil - 1, ALU.bitwise_and))
                link(dve.tensor_copy(resid_f, resid_i))
                link(dve.scalar_tensor_tensor(bias_t[:, g, :], resid_f, MASKED, dist, ALU.mult, ALU.add))
                for cmp, lim in ((ALU.is_gt, 0.0), (ALU.is_lt, float(-window))):
                    if lim <= -T:
                        continue
                    link(dve.tensor_single_scalar(resid_f, dist, lim, cmp))
                    link(dve.scalar_tensor_tensor(bias_t[:, g, :], resid_f, MASKED, bias_t[:, g, :],
                                                  ALU.mult, ALU.add))

            def attention(i, n_next):
                for s in range(CH):
                    low(3 * i + 1, s, W_A)
                dve.wait_ge(aoT_hi, i + 1)
                dve.tensor_tensor(oAT[:, 1, bass.ds(i, 1), :].rearrange("p a t -> p (a t)"), bank(7, T),
                                  oAT[:, 0, bass.ds(i, 1), :].bitcast(F32).rearrange("p a t -> p (a t)"),
                                  ALU.subtract).then_inc(aoT_lo, 1)
                for s in range(CH):
                    if s == CH - 1:
                        dve.wait_ge(chunk_used, CH * (3 * i + 2))
                        dve.tensor_copy(kT.rearrange("p g t -> p (g t)"), banks(2, NG * T)).then_inc(ak_ev, 1)
                    low(3 * i + 2, s, W_A)
                for u in range(4):
                    span = T if u % 2 == 0 else P
                    dve.wait_ge(as_done, 4 * i + u + 1)
                    dve.scalar_tensor_tensor(probs[u].rearrange("p (g s) -> p g s", g=NG),
                                             bias_t[:, :, T - span:T], slope[:, u // 2:u // 2 + 1],
                                             s_cols(u).rearrange("p (g s) -> p g s", g=NG),
                                             ALU.mult, ALU.add).then_inc(as_chain, 1)
                    dve.wait_ge(as_chain, 4 * i + u + 1)
                    dve.tensor_reduce(negmax[:, u:u + 1], probs[u], AX_X, ALU.max, negate=True).then_inc(as_ready, 1)
                dve.tensor_scalar(slope[:, :], slope[:, :], 2.0 ** (-16.0 / HEADS), None, ALU.mult).then_inc(slope_chain, 1)
                for s in range(CH):
                    if s == CH - 1:
                        dve.wait_ge(chunk_used, CH * (3 * i + 3))
                        dve.tensor_copy(vA.rearrange("p a g n -> p a (g n)"), ps[:, 0:2, 0:NG * P]).then_inc(av_ev, 1)
                    low(3 * i + 3, s, n_next)
                for u in (1, 3):
                    dve.wait_ge(apt_done, 4 * i + u + 1)
                    dve.tensor_copy(probsT[u], s_cols(u)).then_inc(apt_dve, 1)
                dve.wait_ge(ap_ready, 4 * i + 4)
                dve.reciprocal(rden[:, :], den[:, :]).then_inc(ao_rden, 1)
                dve.wait_ge(ao_rden, i + 1)
                dve.wait_ge(ao_done, i + 1)
                for u in range(4):
                    j, t = u // 2, 1 - u % 2
                    ins = dve.tensor_scalar(oA[:, t, j * HEAD_DIM:(j + 1) * HEAD_DIM],
                                            ps[:, 6, t * P + j * HEAD_DIM:t * P + (j + 1) * HEAD_DIM],
                                            rden[:, u:u + 1], None, ALU.mult)
                ins.then_inc(ao_ev, 1)
                dve.wait_ge(slope_chain, i + 1)

            with dve.Fori(0, PAIRS - 1) as i:
                attention(i, W_A)
            attention(PAIRS - 1, W_R)
            dve.wait_ge(aoT_hi, PAIRS + 1)
            dve.tensor_tensor(oAT[:, 1, 0, :], bank(7, T), oAT[:, 0, 0, :].bitcast(F32), ALU.subtract).then_inc(aoT_lo, 1)
            dve.memset(oR, 0.0).then_inc(r_out, 1)
            dve.wait_ge(decay_done, RET_HEADS)

            def retention(i, n_next):
                for s in range(CH):
                    low(Q_RET + 1 + 3 * i, s, W_R)
                dve.wait_ge(roT_hi, i + 1)
                dve.tensor_tensor(oRT[:, 1, bass.ds(2 * i, 2), :].rearrange("p a t -> p (a t)"), bank(5),
                                  oRT[:, 0, bass.ds(2 * i, 2), :].bitcast(F32).rearrange("p a t -> p (a t)"),
                                  ALU.subtract).then_inc(roT_lo, 1)
                for s in range(CH):
                    low(Q_RET + 2 + 3 * i, s, W_R)
                dve.wait_ge(rat_done, i + 1)
                for c, n in ((0, T), (T, P)):
                    ins = dve.scalar_tensor_tensor(attR[:, c:c + n], ps[:, 3, c:c + n], float(RK) ** -0.5,
                                                   decay[:, bass.ds(i, 1), 0:n].rearrange("p a n -> p (a n)"),
                                                   ALU.mult, ALU.mult)
                ins.then_inc(rat_ev, 1)
                for s in range(CH):
                    low(Q_RET + 3 + 3 * i, s, n_next)
                dve.wait_ge(ry_done, i + 1)
                for t in range(TT):
                    dve.bn_stats(stats[:, t, :], ps[:, 4, t * RV:(t + 1) * RV]).then_inc(r_stats, 1)
                dve.wait_ge(r_stats, TT * i + TT)
                dve.tensor_copy(gap[:, :], half_neg[:, :]).then_inc(r_gap, 1)
                for t in range(TT):
                    dve.bn_aggr(meanvar[:, t, :], stats[:, t, :]).then_inc(r_aggr, 1)
                dve.wait_ge(r_aggr, TT * i + TT)
                dve.tensor_scalar(meanvar[:, :, 1], meanvar[:, :, 1], EPS, None, ALU.add).then_inc(rvar, 1)
                dve.wait_ge(rrstd, i + 1)
                for t in range(TT):
                    ins = dve.tensor_scalar(oR[:, t, :], ps[:, 4, t * RV:(t + 1) * RV], meanvar[:, t, 0:1],
                                            rstdR[:, t:t + 1], ALU.subtract, ALU.mult)
                ins.then_inc(r_norm, 1)
                dve.wait_ge(r_norm, i + 1)
                dve.wait_ge(r_swish, i + 1)
                dve.tensor_tensor(oR, oR, swish, ALU.mult).then_inc(r_out, 1)

            with dve.Fori(0, RET_HEADS - 1) as i:
                retention(i, W_R)
            retention(RET_HEADS - 1, W_G)
            with dve.Fori(0, GI) as i:
                for s in range(CH):
                    low(Q_GATE + 1 + i, s, W_G)
            dve.wait_ge(roT_hi, RET_HEADS + 1)
            dve.tensor_tensor(oRT[:, 1, 0:2, :].rearrange("p a t -> p (a t)"), bank(5),
                              oRT[:, 0, 0:2, :].bitcast(F32).rearrange("p a t -> p (a t)"),
                              ALU.subtract).then_inc(roT_lo, 1)

            for s in range(CH):
                low(Q_WRET, s, W_B)
            dve.wait_ge(g_ready, 2 * GI)
            for b in range(KT // 2):
                if b < KT // 2 - 1:
                    dve.wait_ge(bA_done, b + 1)
                else:
                    dve.wait_ge(chunk_used, CH * (Q_ATTN + 1))
                dve.tensor_tensor(merged[:, 2 * b:2 * b + 2, :], ps[:, 4 + b, :].rearrange("p (c t) -> p c t", c=2),
                                  gateA[:, 2 * b:2 * b + 2, :], ALU.mult).then_inc(bA_ev, 1)
            for Q in (Q_WRET + 1, Q_OUT):
                for s in range(CH):
                    low(Q, s, W_B)
            dve.wait_ge(bA_ev, KT // 2)
            for b in range(KT // 2):
                tiles = slice(2 * b, 2 * b + 2)
                if b < KT // 2 - 1:
                    dve.wait_ge(bR_done, b + 1)
                else:
                    dve.wait_ge(chunk_used, CH * (Q_WRET + 2))
                dve.tensor_tensor(mtmp, ps[:, b, :].rearrange("p (c t) -> p c t", c=2), gateR[:, tiles, :],
                                  ALU.mult).then_inc(b_tmp, 1)
                dve.wait_ge(b_tmp, b + 1)
                dve.tensor_tensor(merged[:, tiles, :], merged[:, tiles, :], mtmp, ALU.add).then_inc(b_sum, 1)
                dve.wait_ge(b_hi, b + 1)
                dve.tensor_tensor(hT[:, 1, tiles, :], merged[:, tiles, :], hT[:, 0, tiles, :].bitcast(F32),
                                  ALU.subtract).then_inc(b_ready, 1)
            for s in range(CH):
                low(Q_OUT + 1, s, W_B)

            mean_square(1)
            dve.wait_ge(s_gain, 32)
            dve.wait_ge(rstd_done, 2)
            for t in range(TT):
                dve.scalar_tensor_tensor(hn[:, t, :, :], permuted(banks(4 + 2 * t)), rstd[:, 1, t:t + 1],
                                         permuted(gain[:, :]), ALU.mult, ALU.mult).then_inc(hn_done, 1)
            dve.wait_ge(hT_psum, 4)
            dve.tensor_copy(h2T[:, 4:8, :].rearrange("p k t -> p (k t)"), banks(2)).then_inc(hT_dve, 1)
            dve.wait_ge(s_wr, 32)
            dve.wait_ge(logits_done, 1)
            dve.wait_ge(const_ready, 7)

            def per_row(k, n):
                return r1[:, k, :].unsqueeze(2).to_broadcast([P, TT, n])

            lp = ps[:, 0, 0:TT * 64].rearrange("p (a n) -> p a n", a=TT)[:, :, 0:NR]
            link(dve.tensor_tensor(lg[:, :, :], lp, br[:, :].unsqueeze(1).to_broadcast([P, TT, NR]), ALU.add))
            gl, el = lg[:, :, 0:N_GROUPS], lg[:, :, N_GROUPS:NR]
            rga, rgb = ra[:, :, 0:N_GROUPS], rb[:, :, 0:N_GROUPS]
            link(dve.tensor_reduce(r1[:, 0, :], gl, AX_X, ALU.max))
            link(dve.tensor_tensor(rb[:, :, 0:N_GROUPS], gl, per_row(0, N_GROUPS), ALU.is_equal))
            dve.tensor_tensor(rga, gl, per_row(0, N_GROUPS), ALU.subtract).then_inc(d_route, 1)

            def first_of(hits, n, k, dst):
                ids = rev_ids[:, 0:n].unsqueeze(1).to_broadcast([P, TT, n])
                link(dve.tensor_tensor(hits, hits, ids, ALU.mult))
                link(dve.tensor_reduce(r1[:, k, :], hits, AX_X, ALU.max))
                link(dve.tensor_tensor(dst, hits, per_row(k, n), ALU.is_equal))

            first_of(rgb, N_GROUPS, 1, rgb)
            link(dve.tensor_scalar(rgb, rgb, 1.0, -MASKED, ALU.subtract, ALU.mult))
            for t in range(TT):
                link(dve.tensor_tensor(el[:, t, :].rearrange("p (g n) -> p g n", g=N_GROUPS),
                                       el[:, t, :].rearrange("p (g n) -> p g n", g=N_GROUPS),
                                       rgb[:, t, :].unsqueeze(2).to_broadcast([P, N_GROUPS, PER_GROUP]), ALU.add))
            rbe = rb[:, :, N_GROUPS:NR]
            link(dve.tensor_reduce(r1[:, 3, :], el, AX_X, ALU.max))
            link(dve.tensor_tensor(rbe, el, per_row(3, E), ALU.is_equal))
            first_of(rbe, E, 7, oh1[:, :, :])
            link(dve.scalar_tensor_tensor(el, oh1[:, :, :], 2 * MASKED, el, ALU.mult, ALU.add))
            link(dve.tensor_reduce(r1[:, 4, :], el, AX_X, ALU.max))
            link(dve.tensor_tensor(rbe, el, per_row(4, E), ALU.is_equal))
            first_of(rbe, E, 8, oh2[:, :, :])
            dve.tensor_tensor(r1[:, 5, :], r1[:, 4, :], r1[:, 3, :], ALU.subtract).then_inc(d_route, 1)
            link(dve.tensor_tensor(sel[:, :, :], oh1[:, :, :], oh2[:, :, :], ALU.add))
            dve.tensor_tensor(sel_all[:, :], sel[:, 0, :], sel[:, 1, :], ALU.add).then_inc(sel_ready, 1)
            dve.wait_ge(gexp, TT)
            dve.wait_ge(e2exp, 1)
            link(dve.tensor_scalar(r1[:, 9, :], r1[:, 6, :], 1.0, None, ALU.add))
            link(dve.tensor_tensor(r1[:, 9, :], r1[:, 9, :], r1[:, 2, :], ALU.mult))
            link(dve.reciprocal(r1[:, 10, :], r1[:, 9, :]))
            link(dve.tensor_tensor(r1[:, 11, :], r1[:, 10, :], r1[:, 6, :], ALU.mult))
            link(dve.tensor_tensor(oh1[:, :, :], oh1[:, :, :], per_row(10, E), ALU.mult))
            link(dve.tensor_tensor(oh2[:, :, :], oh2[:, :, :], per_row(11, E), ALU.mult))
            link(dve.tensor_tensor(gate[:, :, :], oh1[:, :, :], oh2[:, :, :], ALU.add))
            dve.wait_ge(pos_done, 1)
            link(dve.tensor_copy(cnt[:, 0:2, :], ps[0:1, 2, 0:E].rearrange("p (n j) -> p j n", j=2)))
            link(dve.tensor_tensor(cnt[:, 2, :], cnt[:, 0, :], cnt[:, 1, :], ALU.max))
            link(dve.memset(sched_f[:, 0, :], 1.0))
            for r in range(1, ROUNDS):
                link(dve.scalar_tensor_tensor(sched_f[:, 0, :], cnt[:, 2, :], float(r * SLOTS), sched_f[:, 0, :],
                                              ALU.is_gt, ALU.add))
            link(dve.memset(sched_f[:, 1, 0:1], 0.0))
            link(dve.tensor_copy(sched_f[:, 1, 1:NP], sched_f[:, 0, 0:NP - 1]))
            a, b, step = 1, 2, 1
            while step < NP:
                link(dve.tensor_copy(sched_f[:, b, 0:step], sched_f[:, a, 0:step]))
                link(dve.tensor_tensor(sched_f[:, b, step:NP], sched_f[:, a, step:NP], sched_f[:, a, 0:NP - step], ALU.add))
                a, b, step = b, a, 2 * step
            link(dve.tensor_copy(sched[:, 0, :], sched_f[:, 0, :]))
            dve.tensor_copy(sched[:, 1, :], sched_f[:, a, :]).then_inc(sched_ready, 1)
            pp = ps[:, 1, 0:TT * E].rearrange("p (a n) -> p a n", a=TT)
            link(dve.scalar_tensor_tensor(pos[:, :, :], pp, 1.0, sel[:, :, :], ALU.add, ALU.mult))
            link(dve.tensor_scalar(pos[:, :, :], pos[:, :, :], 1.0, None, ALU.subtract))
            dve.memset(gatedT[:, :], 0.0).then_inc(pgt_ev, 1)
            for h in range(2):
                dve.memset(yS[:, h * HALF:(h + 1) * HALF], 0.0).then_inc(yS_ev[h], 1)

            dve.wait_ge(sched_ready, 1)
            with dve.Fori(0, NP) as p:
                R = dve.value_load(sched[0:1, 0, bass.ds(p, 1)], min_val=1, max_val=ROUNDS)
                C = dve.value_load(sched[0:1, 1, bass.ds(p, 1)], min_val=0, max_val=ROUNDS * NP)
                with dve.Fori(0, R) as r:
                    n = C + r
                    ids = slot_ids[:, bass.ds(r * SLOTS, SLOTS)]

                    def mine(table, t, j):
                        return table[:, t, bass.ds(2 * p + j, 1)]

                    for t in range(TT):
                        for j in range(2):
                            ins = dve.tensor_scalar(onehot[:, t, j * SLOTS:(j + 1) * SLOTS], ids, mine(pos, t, j), None,
                                                    ALU.is_equal)
                    ins.then_inc(P_built, 1)
                    for t in range(TT):
                        for j in range(2):
                            ins = dve.tensor_scalar(gated[:, t, j * SLOTS:(j + 1) * SLOTS], ids, mine(pos, t, j),
                                                    mine(gate, t, j), ALU.is_equal, ALU.mult)
                    ins.then_inc(Pg_built, 1)
                    dve.wait_ge(gather_hi, n + 1)
                    dve.tensor_copy(xg[:, 4:8, :].rearrange("p k s -> p (k s)"), bank(1)).then_inc(xg_dve, 1)
                    dve.wait_ge(silu_done, n + 1)
                    dve.wait_ge(up_done, n + 1)
                    dve.tensor_tensor(hid, sg, bank(3), ALU.mult).then_inc(hid_ready, 1)
                    dve.wait_ge(pgt_done, n + 1)
                    dve.tensor_copy(gatedT[:, :], bank(1, T)).then_inc(pgt_ev, 1)

            mean_square(2)
            dve.wait_ge(s_gain, 48)
            dve.wait_ge(rstd_done, 3)
            for t in range(TT):
                dve.scalar_tensor_tensor(res[:, t, :], banks(4 + 2 * t), rstd[:, 2, t:t + 1], gain[:, :],
                                         ALU.mult, ALU.mult).then_inc(fin, 1)

        @block.tensor
        def _(pe):
            def mm(o, l, r, start, stop, shared=False):
                return pe.matmul(o, lhsT=l, rhs=r, start=start, stop=stop, skip_group_check=shared)

            def mm3(o, l, r, start):
                mm(o, l[0], r[0], start, False, True)
                mm(o, l[0], r[1], False, False, True)
                return mm(o, l[1], r[0], False, False, True)

            def transpose_rows(n):
                pe.wait_ge(hn_done, 2 * n + 2)
                for k in range(KT):
                    for t in range(TT):
                        ins = pe.transpose(ps[:, k // 2, (k % 2) * T + t * P:(k % 2) * T + (t + 1) * P],
                                           hn[:, t, k, :], ident[:, :])
                    if k in (3, 7):
                        ins.then_inc(hT_psum, 1)

            def quad(Q, n, steps, use):
                for s in range(CH):
                    pe.wait_ge(lo_ready, CH * Q + s + 1)
                    ins = use(s, parts(s, n, steps))
                    ins.then_inc(chunk_used, 1)

            def columns(n_tiles, b, w_words):
                def use(s, w):
                    for kk in range(2):
                        k = 2 * s + kk
                        for c in range(n_tiles):
                            o = ps[:, b + c // 2, (c % 2) * T:(c % 2 + 1) * T]
                            ins = mm3(o, [w[a][:, kk, c * P:(c + 1) * P] for a in range(2)],
                                      [hT[:, a, k, :] for a in range(2)], k == 0 and c % 2 == 0)
                    return ins
                return use

            def rows(outs, own_bank):
                def use(s, w):
                    for kk in range(2):
                        k = 2 * s + kk
                        for t in range(TT):
                            ins = mm3(outs[t], [hT[:, a, k, t * P:(t + 1) * P] for a in range(2)],
                                      [w[a][:, kk, :] for a in range(2)], k == 0 and (own_bank or t == 0))
                    return ins
                return use

            pe.wait_ge(const_ready, 1)
            transpose_rows(0)
            pe.wait_ge(hT_act, 2)
            pe.wait_ge(hT_dve, 2)

            def transpose_attn(i):
                pe.wait_ge(ao_ev, i + 1)
                for t in range(TT):
                    ins = pe.transpose(ps[:, 7, t * P:(t + 1) * P], oA[:, t, :], ident[:, :])
                ins.then_inc(aoT_done, 1)

            with pe.Fori(0, PAIRS) as i:
                quad(3 * i, W_A, 2, columns(NG, 0, W_A))
                quad(3 * i + 1, W_A, 2, columns(NG, 2, W_A))
                transpose_attn(i)
                pe.wait_ge(aq_ev, i + 1)
                pe.wait_ge(ak_ev, i + 1)
                for u in range(4):
                    j, t = u // 2, 1 - u % 2
                    h0, span = j * HEAD_DIM, (t + 1) * P
                    if u == 3:
                        pe.wait_ge(aoT_lo, i + 2)
                    for g in range(NG):
                        ins = mm(s_cols(u)[:, g * span:(g + 1) * span], qT[h0:h0 + HEAD_DIM, g, t * P:(t + 1) * P],
                                 kT[h0:h0 + HEAD_DIM, g, 0:span], True, True)
                    ins.then_inc(as_done, 1)
                quad(3 * i + 2, W_A, 2, rows([bank(0, NG * P), bank(1, NG * P)], True))
                for u in range(4):
                    pe.wait_ge(ap_ready, 4 * i + u + 1)
                    for c in range(UC[u % 2] // P):
                        ins = pe.transpose(s_cols(u)[:, c * P:(c + 1) * P], probs[u][:, c * P:(c + 1) * P], ident[:, :])
                    ins.then_inc(apt_done, 1)
                pe.wait_ge(av_ev, i + 1)
                pe.wait_ge(apt_dve, 2 * i + 1)
                for u in range(4):
                    j, t = u // 2, 1 - u % 2
                    if u % 2 == 0:
                        pe.wait_ge(apt_act, 2 * i + u // 2 + 1)
                    else:
                        pe.wait_ge(apt_dve, 2 * i + u // 2 + 1)
                    n_blocks = UC[u % 2] // P
                    for c in range(n_blocks):
                        g, s = c // (t + 1), c % (t + 1)
                        ins = mm(ps[:, 6, t * P + j * HEAD_DIM:t * P + (j + 1) * HEAD_DIM],
                                 probsT[u][:, c * P:(c + 1) * P], vA[:, s, g, j * HEAD_DIM:(j + 1) * HEAD_DIM],
                                 c == 0, c == n_blocks - 1)
                ins.then_inc(ao_done, 1)
            transpose_attn(PAIRS)

            def transpose_ret(i):
                pe.wait_ge(r_out, i + 1)
                pe.wait_ge(roT_lo, i + 1)
                for c in range(2):
                    for t in range(TT):
                        ins = pe.transpose(ps[:, 5, c * T + t * P:c * T + (t + 1) * P], oR[:, t, c * P:(c + 1) * P],
                                           ident[:, :])
                ins.then_inc(roT_done, 1)

            with pe.Fori(0, RET_HEADS) as i:
                quad(Q_RET + 3 * i, W_R, 2, columns(2, 0, W_R))
                transpose_ret(i)
                quad(Q_RET + 1 + 3 * i, W_R, 2, rows([ps[:, 2, t * RV:(t + 1) * RV] for t in range(TT)], False))
                pe.wait_ge(rqk_ev, i + 1)
                mm(ps[:, 3, 0:T], qkR[:, 1, 0:P], qkR[:, 0, :], True, True)
                mm(ps[:, 3, T:T + P], qkR[:, 1, P:T], qkR[:, 0, P:T], True, True).then_inc(rat_done, 1)
                quad(Q_RET + 2 + 3 * i, W_R, 2, rows([ps[:, 1, t * RV:(t + 1) * RV] for t in range(TT)], False))
                pe.wait_ge(rat_ev, i + 1)
                pe.wait_ge(rv_ev, i + 1)
                mm(ps[:, 4, 0:RV], attR[:, 0:P], vR[:, 0, :], True, True)
                mm(ps[:, 4, RV:2 * RV], attR[:, P:2 * P], vR[:, 0, :], True, False)
                mm(ps[:, 4, RV:2 * RV], attR[:, 2 * P:3 * P], vR[:, 1, :], False, True).then_inc(ry_done, 1)

            quad(Q_GATE, W_G, 2, columns(4, 0, W_G))
            transpose_ret(RET_HEADS)
            quad(Q_GATE + 1, W_G, 2, columns(4, 2, W_G))
            with pe.Fori(1, GI // 2) as i:
                for m in range(2):
                    pe.wait_ge(g_ready, 4 * i - 2 + 2 * m)
                    quad(Q_GATE + m + 2 * i, W_G, 2, columns(4, 2 * m, W_G))

            def branch(outs_from, c0, tile_of, oT, n_c, done):
                def use(s, w):
                    c = c0 + s
                    for j in range(KT):
                        ins = mm3(ps[:, outs_from + j // 2, (j % 2) * T:(j % 2 + 1) * T],
                                  [w[a][:, 0, j * P:(j + 1) * P] for a in range(2)],
                                  [oT[:, a, tile_of(c), :] for a in range(2)], c == 0 and j % 2 == 0)
                        if c == n_c - 1 and j % 2 == 1 and j < KT - 1:
                            ins.then_inc(done, 1)
                    return ins
                return use

            pe.wait_ge(aoT_lo, PAIRS + 2)
            pe.wait_ge(roT_lo, RET_HEADS + 2)
            quad(Q_ATTN, W_B, 1, branch(4, 0, lambda c: (c + 1) % PAIRS, oAT, PAIRS, bA_done))
            pe.wait_ge(g_ready, 2 * GI)
            for m in range(2):
                quad(Q_WRET + m, W_B, 1, branch(0, CH * m, lambda c: (c + 2) % (2 * RET_HEADS), oRT,
                                                2 * RET_HEADS, bR_done))

            pe.wait_ge(bA_ev, KT // 2)
            for t in range(TT):
                for h in range(2):
                    mm(ps[:, 4 + 2 * t + h, :], ident[:, :], xs[:, t, h * HALF:(h + 1) * HALF], True, False, True)

            def project_out(j0):
                def use(s, w):
                    j = j0 + s
                    pe.wait_ge(b_ready, j // 2 + 1)
                    for t in range(TT):
                        for h in range(2):
                            ins = mm3(ps[:, 4 + 2 * t + h, :], [hT[:, a, j, t * P:(t + 1) * P] for a in range(2)],
                                      [w[a][:, 0, h * HALF:(h + 1) * HALF] for a in range(2)], False)
                    return ins
                return use

            quad(Q_OUT, W_B, 1, project_out(0))
            quad(Q_OUT + 1, W_B, 1, project_out(CH))

            transpose_rows(1)
            pe.wait_ge(hT_act, 3)
            pe.wait_ge(hT_dve, 3)
            pe.wait_ge(s_wr, 32)
            for t in range(TT):
                for k in range(KT):
                    ins = mm(ps[:, 0, t * 64:t * 64 + NR], h2T[:, k, t * P:(t + 1) * P], wr[:, k, :], k == 0, k == KT - 1)
            ins.then_inc(logits_done, 1)
            pe.wait_ge(sel_ready, 1)
            pe.wait_ge(const_ready, 7)
            mm(ps[:, 1, 0:E], before[:, :], sel[:, 0, :], True, True)
            mm(ps[:, 1, E:2 * E], ones[:, :], sel[:, 0, :], True, False)
            mm(ps[:, 1, E:2 * E], before[:, :], sel[:, 1, :], False, True)
            mm(ps[0:1, 2, 0:E], ones[:, 0:1], sel_all[:, :], True, True).then_inc(pos_done, 1)

            def scatter(h):
                for t in range(TT):
                    ins = mm(ps[:, 4 + 2 * t + h, :], gatedT[:, t * P:(t + 1) * P], yS[:, h * HALF:(h + 1) * HALF],
                             False, False, True)
                ins.then_inc(scatter_done, 1)

            def both(b, w, steps, left, cols):
                for k in range(steps):
                    for j in range(2):
                        ins = mm(ps[j * SLOTS:(j + 1) * SLOTS, b, :], left[:, k, j * SLOTS:(j + 1) * SLOTS],
                                 w[j][:, k, cols], k == 0, k == steps - 1)
                return ins

            pe.wait_ge(sched_ready, 1)
            with pe.Fori(0, NP) as p:
                R = pe.value_load(sched[0:1, 0, bass.ds(p, 1)], min_val=1, max_val=ROUNDS)
                C = pe.value_load(sched[0:1, 1, bass.ds(p, 1)], min_val=0, max_val=ROUNDS * NP)
                with pe.Fori(0, R) as r:
                    n = C + r
                    pe.wait_ge(P_built, n + 1)
                    pe.wait_ge(pgt_ev, n + 1)
                    for k in range(KT):
                        for t in range(TT):
                            ins = mm(ps[:, k // 4, (k % 4) * P:(k % 4 + 1) * P], hn[:, t, k, :], onehot[:, t, :],
                                     t == 0, t == TT - 1)
                        if k in (3, 7):
                            ins.then_inc(gather_lo if k == 3 else gather_hi, 1)
                    pe.wait_ge(yS_ev[0], n + 1)
                    scatter(0)
                    pe.wait_ge(xg_act, n + 1)
                    pe.wait_ge(xg_dve, n + 1)
                    pe.wait_ge(s_e[0], 16 * p + 16)
                    pe.wait_ge(s_e[1], 16 * p + 16)
                    both(2, pair_gate, KT, xg, slice(0, FF)).then_inc(gate_done, 1)
                    pe.wait_ge(yS_ev[1], n + 1)
                    pe.wait_ge(s_e[2], 16 * p + 16)
                    pe.wait_ge(s_e[3], 16 * p + 16)
                    both(3, pair_up, KT, xg, slice(0, FF)).then_inc(up_done, 1)
                    scatter(1)
                    pe.wait_ge(hid_ready, n + 1)
                    for f in range(FT):
                        ins = pe.transpose(ps[:, 0, f * P:(f + 1) * P], hid[:, f * P:(f + 1) * P], ident[:, :])
                    ins.then_inc(hidT_done, 1)
                    pe.wait_ge(Pg_built, n + 1)
                    for t in range(TT):
                        ins = pe.transpose(ps[:, 1, t * P:(t + 1) * P], gated[:, t, :], ident[:, :])
                    ins.then_inc(pgt_done, 1)
                    pe.wait_ge(hidT_ev, n + 1)
                    pe.wait_ge(s_e[4], 16 * p + 16)
                    pe.wait_ge(s_e[5], 16 * p + 16)
                    for h in range(2):
                        both(2 + h, pair_down, FT, hidT, slice(h * HALF, (h + 1) * HALF)).then_inc(down_done[h], 1)
            CL = pe.value_load(sched[0:1, 1, NP - 1:NP], min_val=0, max_val=ROUNDS * NP)
            RL = pe.value_load(sched[0:1, 0, NP - 1:NP], min_val=1, max_val=ROUNDS)
            n = CL + RL
            pe.wait_ge(pgt_ev, n + 1)
            for h in range(2):
                pe.wait_ge(yS_ev[h], n + 1)
                scatter(h)


_OUT = (1, 256, 1024)


def kernel(x, g_mix, w_in, w_attn_branch, w_ret_branch, w_out, g_ffn, w_group_router, b_group_router,
           w_expert_router, b_expert_router, w_gate, w_up, w_down, g_final):
    import concourse.bacc as _bacc
    from concourse.bass_utils import run_bass_kernel_spmd as _run

    nc = _bacc.Bacc("TRN2", target_bir_lowering=False, num_devices=1)
    given = {
        "x": np.asarray(x)[0],
        "g_mix": np.asarray(g_mix)[0],
        "w_in": np.asarray(w_in)[0],
        "w_attn": np.asarray(w_attn_branch)[0],
        "w_ret": np.asarray(w_ret_branch)[0],
        "w_out": np.asarray(w_out)[0],
        "g_ffn": np.asarray(g_ffn)[0],
        "w_router": np.concatenate([np.asarray(w_group_router)[0], np.asarray(w_expert_router)[0]], axis=1),
        "b_router": np.concatenate([np.asarray(b_group_router)[0], np.asarray(b_expert_router)[0]]),
        "w_gate": np.asarray(w_gate)[0],
        "w_up": np.asarray(w_up)[0],
        "w_down": np.asarray(w_down)[0],
        "g_final": np.asarray(g_final),
    }
    arrays = {f"in_{n}": np.ascontiguousarray(a) for n, a in given.items()}
    aps = {n: nc.dram_tensor(f"in_{n}", arrays[f"in_{n}"].shape, mybir.dt.from_np(arrays[f"in_{n}"].dtype),
                             kind="ExternalInput").ap() for n in given}
    out = nc.dram_tensor("out_0", _OUT[1:], F32, kind="ExternalOutput").ap()
    hybrid_block(nc, out=out, **aps)
    r = _run(nc, [arrays], core_ids=[0])
    return r.results[0]["out_0"].reshape(_OUT)
```

```python
from contextlib import ExitStack

import numpy as np

import concourse.bass as bass
from concourse import mybir

ALU = mybir.AluOpType
ACT = mybir.ActivationFunctionType
AX_X = mybir.AxisListType.X
F32 = mybir.dt.float32
F32R = mybir.dt.float32r
I32 = mybir.dt.int32

P = 128
GROUPS = ((128, 1), (512, 4), (2048, 16))
HEADS = 8
HEAD_DIM = 64
RET_HEADS = 4
N_GROUPS = 4
PER_GROUP = 8
EPS = 1e-6
SLOTS = 64
MASKED = -1e30
RING = 6


def chain(eng, sem, base):
    count = [0]

    def link(ins):
        count[0] += 1
        ins.then_inc(sem, 1)
        eng.wait_ge(sem, base + count[0])

    return link, count


def hybrid_block(nc, x, g_mix, w_in, w_attn, w_ret, w_out, g_ffn, w_router, b_router,
                 w_gate, w_up, w_down, g_final, out):
    T, D = x.shape
    TT = T // P
    KT = D // P
    NG = len(GROUPS)
    AW = HEADS * HEAD_DIM
    RK = D // 8
    RV = 2 * RK
    E, _, FF = w_gate.shape
    FT = FF // P
    NP = E // 2
    PAIRS = HEADS // 2
    NR = N_GROUPS + E
    ROUNDS = T // SLOTS
    CYCLE = 5
    CH = 4
    SLOT_N = 10
    HALF = D // 2
    assert NP % CYCLE == 1 and 6 * CYCLE % SLOT_N == 0
    assert TT == 2 and KT == 8 and RK == P and HALF == 512 and FT * P == 512 and E == N_GROUPS * PER_GROUP

    COL_Q, COL_K, COL_V = 0, NG * AW, 2 * NG * AW
    COL_RQ = 3 * NG * AW
    COL_RK = COL_RQ + RET_HEADS * RK
    COL_RV = COL_RK + RET_HEADS * RK
    COL_RG = COL_RV + RET_HEADS * RV
    COL_GA = COL_RG + RET_HEADS * RV
    COL_GR = COL_GA + D
    w_in_v = w_in.rearrange("(p k) n -> p k n", k=KT)
    wattn_v = w_attn.rearrange("(c p) n -> p c n", p=P)
    wret_v = w_ret.rearrange("(c p) n -> p c n", p=P)
    wout_v = w_out.rearrange("(c p) n -> p c n", p=P)
    wg_v = w_gate.rearrange("e (p k) f -> e p (k f)", k=KT)
    wu_v = w_up.rearrange("e (p k) f -> e p (k f)", k=KT)
    wd_v = w_down.rearrange("e (c p) d -> e p c d", p=P)
    attn_v = [w_in_v[:, :, c:c + NG * AW].rearrange("p k (g n) -> p k g n", g=NG) for c in (COL_Q, COL_K, COL_V)]
    qk_v = w_in_v[:, :, COL_RQ:COL_RV].rearrange("p k (h n) -> p k h n", h=2)
    gates_v = w_in_v[:, :, COL_GA:COL_GA + 2 * D].rearrange("p k (h n) -> p k h n", h=2)
    x_v = x.rearrange("(a p) d -> p a d", p=P)
    out_v = out.rearrange("(a p) d -> p a d", p=P)

    with ExitStack() as ctx:
        def sb(name, shape, dt=F32):
            return ctx.enter_context(nc.sbuf_tensor(name, shape, dt))

        def sem(name):
            return ctx.enter_context(nc.semaphore(name))

        ps = ctx.enter_context(nc.psum_tensor("ps", [P, 8, 512], F32))

        RAW = 1024
        ring_at = -(-nc.sbuf_base // 32) * 32
        ring = sb("ring", [P, 6, 4096])
        split = nc.alloc_sbuf_tensor_at("split", [P, CH, 2, RAW], F32R, offset=ring_at + 4096 * 4)
        store_at = -(-nc.sbuf_base // 32) * 32
        store = sb("store", [P, 4096])
        xs = store[:, 0:TT * D].rearrange("p (a d) -> p a d", a=TT)
        oAT = nc.alloc_sbuf_tensor_at("oAT", [P, 2, PAIRS, T], F32R, offset=store_at + 4 * TT * D)
        hn = sb("hn", [P, TT, KT, P])
        hT_at = -(-nc.sbuf_base // 32) * 32
        hT = sb("hT", [P, 2, KT, T], F32R)
        hT_slot = nc.alloc_sbuf_tensor_at("hT_slot", [P, 4096], F32, offset=hT_at)
        gain = sb("gain", [P, D])
        ident = sb("ident", [P, P])
        before = sb("before", [P, P])
        ones = sb("ones", [P, P])
        bias_t = sb("bias_t", [P, NG, T])
        slope = sb("slope", [P, 2])
        decay = sb("decay", [P, RET_HEADS, T])
        age = sb("age", [P, T])
        half_neg = sb("half_neg", [P, 2])
        slot_ids = sb("slot_ids", [P, ROUNDS * SLOTS])
        rev_ids = sb("rev_ids", [P, NR])
        ss = sb("ss", [P, 3, TT])
        ms = sb("ms", [P, 3, TT])
        rstd = sb("rstd", [P, 3, TT])

        mid = sb("mid", [P, 4096])
        qT = mid[:, 0:2 * NG * T].rearrange("p (j g t) -> p j g t", j=2, g=NG)
        kT = mid[:, 2 * NG * T:3 * NG * T].rearrange("p (g t) -> p g t", g=NG)
        vA = mid[:, 3 * NG * T:3 * NG * T + TT * NG * P].rearrange("p (a g n) -> p a g n", a=TT, g=NG)
        gateA = mid[:, 0:KT * T].rearrange("p (k t) -> p k t", k=KT)
        gateR = mid[:, KT * T:2 * KT * T].rearrange("p (k t) -> p k t", k=KT)

        UC = [NG * T, NG * P]
        work = sb("work", [P, 4 * (UC[0] + UC[1])])

        def carve(at):
            def take(n):
                at[0] += n
                return work[:, at[0] - n:at[0]]
            return take

        take = carve([0])
        probs = [take(UC[u % 2]) for u in range(4)]
        probsT = [take(UC[u % 2]) for u in range(4)]
        take = carve([0])
        junk = take(D)
        dist_i = take(T).bitcast(I32)
        resid_i = take(T).bitcast(I32)
        resid_f = take(T)
        dist = take(T)
        take = carve([0])
        qkR = take(2 * T).rearrange("p (a t) -> p a t", a=2)
        vR = take(TT * RV).rearrange("p (a n) -> p a n", a=TT)
        attR = take(3 * P)
        swish = take(TT * RV).rearrange("p (a n) -> p a n", a=TT)
        take = carve([3072])
        oR = take(TT * RV).rearrange("p (a n) -> p a n", a=TT)
        take = carve([0])
        merged = take(KT * T).rearrange("p (k t) -> p k t", k=KT)
        mtmp = take(2 * T).rearrange("p (k t) -> p k t", k=2)
        take = carve([D])
        h2T = take(KT * T).rearrange("p (k t) -> p k t", k=KT)
        take = carve([0])
        xg = take(KT * P).rearrange("p (k s) -> p k s", k=KT)
        sg = take(FF)
        hid = take(FF)
        hidT = take(FT * P).rearrange("p (f s) -> p f s", f=FT)
        take = carve([D + KT * T])
        yS = take(D)
        take = carve([2 * D + FF])
        onehot = take(TT * P).rearrange("p (a s) -> p a s", a=TT)
        gated = take(TT * P).rearrange("p (a s) -> p a s", a=TT)

        negmax = sb("negmax", [P, 4])
        den = sb("den", [P, 4])
        rden = sb("rden", [P, 4])
        oRT_at = -(-nc.sbuf_base // 32) * 32
        oRT = sb("oRT", [P, 2, 2 * RET_HEADS, T], F32R)
        oRT_slot = nc.alloc_sbuf_tensor_at("oRT_slot", [P, 4096], F32, offset=oRT_at)
        stats = sb("stats", [P, TT, 6])
        meanvar = sb("meanvar", [P, TT, 2])
        rstdR = sb("rstdR", [P, TT])
        gap = sb("gap", [P, 2])

        wr = sb("wr", [P, KT, NR])
        br = sb("br", [P, NR])
        lg = sb("lg", [P, TT, NR])
        ra = sb("ra", [P, TT, NR])
        rb = sb("rb", [P, TT, NR])
        r1 = sb("r1", [P, 12, TT])
        oh1 = sb("oh1", [P, TT, E])
        oh2 = sb("oh2", [P, TT, E])
        gate = sb("gate", [P, TT, E])
        sel = sb("sel", [P, TT, E])
        sel_all = sb("sel_all", [P, E])
        pos = sb("pos", [P, TT, E])
        fuller = sb("fuller", [NP, 1])
        begun = sb("begun", [NP, ROUNDS])
        rounds = sb("rounds", [NP, 1])
        sched = sb("sched", [1, 2, NP], I32)
        gatedT = sb("gatedT", [P, T])
        res = hn[:, :, :, :].rearrange("p a k q -> p a (k q)")

        s_x = [sem(f"s_x{t}") for t in range(TT)]
        s_gain = sem("s_gain")
        s_wr = sem("s_wr")
        raw_loaded = [sem(f"raw_loaded{s}") for s in range(CH)]
        hi_ready, lo_ready, chunk_used = sem("hi_ready"), sem("lo_ready"), sem("chunk_used")
        slot_loaded = [sem(f"slot_loaded{i}") for i in range(SLOT_N)]
        first_down = [sem(f"first_down{i}") for i in range(SLOT_N)]
        early = sem("early")
        second_gate, second_up = sem("second_gate"), sem("second_up")
        second_down, last_down = sem("second_down"), sem("last_down")
        s_out = sem("s_out")
        const_ready = sem("const_ready")
        pool_chain = sem("pool_chain")
        dve_chain = sem("dve_chain")
        sq_done = sem("sq_done")
        ms_done = sem("ms_done")
        rstd_done = sem("rstd_done")
        hn_done = sem("hn_done")
        hT_psum = sem("hT_psum")
        hT_act = sem("hT_act")
        hT_dve = sem("hT_dve")
        zeros_ready = sem("zeros_ready")
        age_done = sem("age_done")
        decay_done = sem("decay_done")

        aq_ev, ak_ev, av_ev = sem("aq_ev"), sem("ak_ev"), sem("av_ev")
        as_done, as_chain, as_ready = sem("as_done"), sem("as_chain"), sem("as_ready")
        slope_chain = sem("slope_chain")
        ap_ready = sem("ap_ready")
        apt_done, apt_act, apt_dve = sem("apt_done"), sem("apt_act"), sem("apt_dve")
        ap_rden, ap_norm = sem("ap_rden"), sem("ap_norm")
        aoT_done, aoT_hi, aoT_lo = sem("aoT_done"), sem("aoT_hi"), sem("aoT_lo")

        rqk_ev, rv_ev = sem("rqk_ev"), sem("rv_ev")
        rat_done, rat_ev = sem("rat_done"), sem("rat_ev")
        ry_done, r_stats, r_gap = sem("ry_done"), sem("r_stats"), sem("r_gap")
        r_aggr, rvar = sem("r_aggr"), sem("rvar")
        rrstd, r_norm, r_swish, r_out = sem("rrstd"), sem("r_norm"), sem("r_swish"), sem("r_out")
        roT_done, roT_hi, roT_lo = sem("roT_done"), sem("roT_hi"), sem("roT_lo")

        g_ready = sem("g_ready")
        bA_done, bR_done, bA_ev, b_tmp, b_sum = (sem("bA_done"), sem("bR_done"), sem("bA_ev"),
                                                 sem("b_tmp"), sem("b_sum"))
        b_hi, b_ready = sem("b_hi"), sem("b_ready")
        logits_done, gexp, e2exp = sem("logits_done"), sem("gexp"), sem("e2exp")
        d_route = sem("d_route")
        weighted = sem("weighted")
        sel_ready, pos_done, sched_ready = sem("sel_ready"), sem("pos_done"), sem("sched_ready")
        cnt_done, rounds_ready, sched_psum = sem("cnt_done"), sem("rounds_ready"), sem("sched_psum")

        P_built, Pg_built = sem("P_built"), sem("Pg_built")
        gather_lo, gather_hi = sem("gather_lo"), sem("gather_hi")
        xg_act, xg_dve = sem("xg_act"), sem("xg_dve")
        gate_quarter, gate_half = sem("gate_quarter"), sem("gate_half")
        gate_done, up_done, silu_done, hid_ready = sem("gate_done"), sem("up_done"), sem("silu_done"), sem("hid_ready")
        hidT_done, hidT_ev = sem("hidT_done"), sem("hidT_ev")
        pgt_done, pgt_ev = sem("pgt_done"), sem("pgt_ev")
        down_done = [sem(f"down_done{h}") for h in range(2)]
        yS_ev = [sem(f"yS_ev{h}") for h in range(2)]
        stream_done = sem("stream_done")
        fin = sem("fin")

        GI = D // 256
        Q_RET = 3 * PAIRS
        Q_GATE = Q_RET + 3 * RET_HEADS
        Q_ATTN = Q_GATE + GI
        Q_WRET = Q_ATTN + PAIRS // CH
        Q_OUT = Q_WRET + 2 * RET_HEADS // CH
        QUADS = Q_OUT + KT // CH
        W_A, W_R, W_G, W_B = 2 * NG * P, 2 * RV, 2 * 512, D

        def raw(s, n):
            return ring[:, 0, s * RAW:s * RAW + n]

        def parts(s, n, steps):
            return [split[:, s, a, 0:n].rearrange("p (k n) -> p k n", k=steps) for a in range(2)]

        slots = [ring[:, s, :] for s in range(6)] + [oRT_slot[:, :], mid[:, :], store[:, :], hT_slot[:, :]]

        def tiles_of(m):
            return [(6 * m + j) % SLOT_N for j in range(6)]

        def loads_of(m, j):
            return sum(tiles_of(a)[b] == tiles_of(m)[j] for a in range(m + 1) for b in range(6))

        def bank(b, n=512):
            return ps[:, b, 0:n]

        def banks(b, n=1024):
            return ps[:, b:b + 2, :].rearrange("p b n -> p (b n)")[:, 0:n]

        def s_cols(u):
            return (banks(4, UC[0]), bank(6, UC[1]), banks(2, UC[0]), bank(7, UC[1]))[u]

        block = ctx.enter_context(nc.Block())

        @block.sync
        def _(sp):
            for t in range(TT):
                sp.dma_start(xs[:, t, :], x_v[:, t, :]).then_inc(s_x[t], 16)
            sp.dma_start(gain[:, :], g_mix.partition_broadcast(P)).then_inc(s_gain, 16)

            def load_quad(Q, piece):
                for s in range(CH):
                    if not isinstance(Q, int) or Q > 0:
                        sp.wait_ge(lo_ready, CH * Q + s + 1 - CH)
                    for m in range(2):
                        sp.dma_start(*piece(s, m)).then_inc(raw_loaded[s], 16)

            def columns_of(view, n_parts, width, i):
                def piece(s, m):
                    dst = raw(s, 2 * n_parts * width).rearrange("p (k g n) -> p k g n", k=2, g=n_parts)
                    return dst[:, m], view[:, 2 * s + m, :, bass.ds(i * width, width)]
                return piece

            def plain_columns(col, width, i):
                def piece(s, m):
                    dst = raw(s, 2 * width).rearrange("p (k n) -> p k n", k=2)
                    return dst[:, m], w_in_v[:, 2 * s + m, bass.ds(col + i * width, width)]
                return piece

            def full_rows(view, c):
                def piece(s, m):
                    return raw(s, D)[:, m * HALF:(m + 1) * HALF], view[:, c + s, m * HALF:(m + 1) * HALF]
                return piece

            def load_pair(i):
                for m in range(3):
                    load_quad(3 * i + m, columns_of(attn_v[m], NG, P, i))

            load_pair(0)
            with sp.Fori(1, PAIRS) as i:
                load_pair(i)
            def quarter(slot, src, i):
                sp.dma_start(ring[:, slot, bass.ds(i * 1024, 1024)], src).then_inc(early, 16)

            with sp.Fori(0, RET_HEADS) as i:
                load_quad(Q_RET + 3 * i, columns_of(qk_v, 2, RK, i))
                quarter(3, wu_v[1][:, bass.ds(i * 1024, 1024)], i)
                load_quad(Q_RET + 1 + 3 * i, plain_columns(COL_RV, RV, i))
                quarter(4, wd_v[0][:, bass.ds(i, 1), :].rearrange("p c n -> p (c n)"), i)
                load_quad(Q_RET + 2 + 3 * i, plain_columns(COL_RG, RV, i))
                quarter(5, wd_v[1][:, bass.ds(i, 1), :].rearrange("p c n -> p (c n)"), i)
            for s in (3, 4, 5):
                sp.sem_inc(slot_loaded[s], 16)
                if s > 3:
                    sp.sem_inc(first_down[s], 32)
            with sp.Fori(0, GI) as i:
                load_quad(Q_GATE + i, columns_of(gates_v, 2, 256, i))
            for Q, view, c in ((Q_ATTN, wattn_v, 0), (Q_WRET, wret_v, 0), (Q_WRET + 1, wret_v, CH),
                               (Q_OUT, wout_v, 0), (Q_OUT + 1, wout_v, CH)):
                load_quad(Q, full_rows(view, c))
            sp.wait_ge(hn_done, TT)
            sp.dma_start(gain[:, :], g_ffn.partition_broadcast(P)).then_inc(s_gain, 16)

            def load_tile(p, m, j):
                slot = tiles_of(m)[j]
                view = (wg_v, wu_v, wd_v)[j // 2]
                src = view[2 * p + j % 2] if isinstance(p, int) else view[bass.ds(2 * p + j % 2, 1)]
                dst = slots[slot]
                if not isinstance(p, int):
                    src = src.rearrange("e p n -> (e p) n")
                sp.dma_start(dst, src).then_inc(slot_loaded[slot], 16)

            sp.wait_ge(chunk_used, CH * (Q_WRET + 2))
            load_tile(1, 1, 0)
            sp.wait_ge(b_ready, KT // 2)
            load_tile(1, 1, 1)
            sp.wait_ge(lo_ready, CH * QUADS)
            load_tile(0, 0, 0)
            sp.wait_ge(chunk_used, CH * QUADS)
            load_tile(0, 0, 1)
            load_tile(0, 0, 2)
            load_tile(1, 1, 2)
            load_tile(1, 1, 3)
            sp.wait_ge(hn_done, 2 * TT)
            sp.dma_start(gain[:, :], g_final.partition_broadcast(P)).then_inc(s_gain, 16)

            sp.wait_ge(sched_ready, 1)

            def rounds_before(p):
                return sp.value_load(sched[0:1, 1, bass.ds(p, 1) if not isinstance(p, int) else slice(p, p + 1)],
                                     min_val=1, max_val=ROUNDS * NP)

            def load_experts(p, m, first=0, halves=False):
                if first == 0:
                    before_last = rounds_before(p - 1)
                    for tiles, view, read, second in (((0, 1), wg_v, up_done, second_gate),
                                                      ((2, 3), wu_v, down_done[1], second_up)):
                        sp.wait_ge(read, before_last)
                        for h in range(2 if halves else 0):
                            for j in tiles:
                                slot, words = tiles_of(m)[j], slice(h * 2048, (h + 1) * 2048)
                                sp.dma_start(slots[slot][:, words], view[2 * p + j % 2][:, words]).then_inc(
                                    second if h else slot_loaded[slot], 16)
                        if not halves:
                            for j in tiles:
                                load_tile(p, m, j)
                last = rounds_before(p)
                for lo, hi, read, loaded in ((0, 1, gate_quarter, first_down), (1, 2, gate_half, first_down),
                                             (2, FT, gate_done, slot_loaded)):
                    sp.wait_ge(read, last)
                    for j in (4, 5):
                        slot, e = tiles_of(m)[j], 2 * p + j % 2
                        steps, cols = slice(lo, hi), slice(0, HALF if halves else D)
                        src = wd_v[e] if isinstance(p, int) else wd_v[bass.ds(e, 1)].rearrange("e p c n -> (e p) c n")
                        sp.dma_start(slots[slot].rearrange("p (c n) -> p c n", c=FT)[:, steps, cols],
                                     src[:, steps, cols]).then_inc(loaded[slot], 16)
                for a in range(2 if halves else 0):
                    for j in (4, 5):
                        steps = slice(2 * a, 2 * a + 2)
                        sp.dma_start(slots[tiles_of(m)[j]].rearrange("p (c n) -> p c n", c=FT)[:, steps, HALF:],
                                     wd_v[2 * p + j % 2][:, steps, HALF:]).then_inc(last_down if a else second_down, 16)

            load_experts(1, 1, first=4)
            for m in range(2, CYCLE):
                load_experts(m, m)
            with sp.Fori(1, NP // CYCLE) as i:
                for m in range(CYCLE):
                    load_experts(CYCLE * i + m, m)
            load_experts(NP - 1, 0, halves=True)

            for t in range(TT):
                for h in range(2):
                    sp.wait_ge(fin, 2 * t + h + 1)
                    cols = slice(h * HALF, (h + 1) * HALF)
                    sp.dma_start(out_v[:, t, cols], res[:, t, cols]).then_inc(s_out, 16)
            sp.wait_ge(s_out, 16 * TT * 2)

        @block.gpsimd
        def _(pool):
            link, _n = chain(pool, pool_chain, 0)
            link(pool.memset(ident[:, :], 0.0))
            pool.affine_select(out=ident[:, :], in_=ident[:, :], compare_op=ALU.not_equal, fill=1.0, base=0,
                               pattern=[[-1, P]], channel_multiplier=1).then_inc(const_ready, 1)
            pool.memset(half_neg[:, :], -0.5).then_inc(const_ready, 1)

            def inv_root(n):
                for t in range(TT):
                    pool.wait_ge(ms_done, TT * n + t + 1)
                    pool.tensor_tensor(out=rstd[:, n, t:t + 1], in0=ms[:, n, t:t + 1], in1=half_neg[:, 0:1],
                                       op=ALU.pow).then_inc(rstd_done, 1)

            pool.wait_ge(const_ready, 2)
            inv_root(0)
            pool.iota(dist_i[:, :], pattern=[[1, T]], base=-P, channel_multiplier=-1).then_inc(const_ready, 1)
            link(pool.iota(age[:, :], pattern=[[1, T]], base=0, channel_multiplier=-1,
                           allow_small_or_imprecise_dtypes=True))
            pool.affine_select(out=age[:, 0:P], in_=age[:, 0:P], compare_op=ALU.is_ge, fill=-MASKED, base=0,
                               pattern=[[1, P]], channel_multiplier=-1).then_inc(age_done, 1)
            link(pool.memset(before[:, :], 1.0))
            pool.affine_select(out=before[:, :], in_=before[:, :], compare_op=ALU.is_gt, fill=0.0, base=0,
                               pattern=[[1, P]], channel_multiplier=-1).then_inc(const_ready, 1)
            pool.memset(ones[:, :], 1.0).then_inc(const_ready, 1)
            pool.iota(slot_ids[:, :], pattern=[[1, ROUNDS * SLOTS]], base=1, channel_multiplier=0,
                      allow_small_or_imprecise_dtypes=True).then_inc(const_ready, 1)
            pool.iota(rev_ids[:, :], pattern=[[-1, NR]], base=NR, channel_multiplier=0,
                      allow_small_or_imprecise_dtypes=True).then_inc(const_ready, 1)
            with pool.Fori(0, RET_HEADS) as i:
                pool.wait_ge(rvar, i + 1)
                pool.tensor_tensor(out=rstdR[:, :], in0=meanvar[:, :, 1], in1=half_neg[:, 0:TT],
                                   op=ALU.pow).then_inc(rrstd, 1)
            inv_root(1)
            inv_root(2)

        @block.scalar
        def _(act):
            act.dma_start(wr[:, :, :], w_router.rearrange("(p k) n -> p k n", k=KT)).then_inc(s_wr, 16)
            act.dma_start(br[:, :], b_router.partition_broadcast(P)).then_inc(s_wr, 16)

            def high(Q, s, n):
                act.wait_ge(raw_loaded[s], 32 * Q + 32)
                if not isinstance(Q, int) or Q > 0:
                    act.wait_ge(chunk_used, CH * Q + s + 1 - CH)
                act.activation(split[:, s, 0, 0:n], raw(s, n), ACT.Copy).then_inc(hi_ready, 1)

            for t in range(TT):
                act.wait_ge(s_x[t], 16)
                if t > 0:
                    act.wait_ge(sq_done, t)
                act.activation(junk, xs[:, t, :], ACT.Square, accum_out=ss[:, 0, t:t + 1]).then_inc(sq_done, 1)

            def transposed_high(t):
                for h in range(2):
                    b = 2 * t + h
                    act.wait_ge(hT_psum, b + 1)
                    act.activation(hT[:, 0, 4 * h:4 * h + 4, t * P:(t + 1) * P],
                                   ps[:, b, :].rearrange("p (k t) -> p k t", k=4), ACT.Copy).then_inc(hT_act, 1)

            high(0, 0, W_A)
            high(0, 1, W_A)
            transposed_high(0)
            transposed_high(1)
            high(0, 2, W_A)
            high(0, 3, W_A)
            act.wait_ge(age_done, 1)
            for h in range(RET_HEADS):
                act.activation(decay[:, h, :], age[:, :], ACT.Exp,
                               scale=float(np.log1p(-2.0 ** (-5.0 - h)))).then_inc(decay_done, 1)

            def attention(i, n_next):
                for s in range(CH):
                    high(3 * i + 1, s, W_A)
                act.wait_ge(chunk_used, CH * (3 * i + 1))
                for j in range(2):
                    rows_j = slice(j * HEAD_DIM, (j + 1) * HEAD_DIM)
                    act.activation(qT[rows_j, j].rearrange("p g t -> p (g t)"), banks(0, NG * T)[rows_j], ACT.Copy,
                                   scale=float(HEAD_DIM) ** -0.5).then_inc(aq_ev, 1)
                for s in range(CH):
                    high(3 * i + 2, s, W_A)
                for u in range(4):
                    act.wait_ge(as_ready, 4 * i + u + 1)
                    act.activation(probs[u], probs[u], ACT.Exp, bias=negmax[:, u:u + 1],
                                   accum_out=den[:, u:u + 1]).then_inc(ap_ready, 1)
                for s in range(2):
                    high(3 * i + 3, s, n_next)
                for n, u in enumerate((0, 2)):
                    act.wait_ge(apt_done, 4 * i + n + 1)
                    act.activation(probsT[u], s_cols(u), ACT.Copy).then_inc(apt_act, 1)
                for s in range(2, CH):
                    high(3 * i + 3, s, n_next)
                act.wait_ge(aoT_done, i + 1)
                at = slice(i, i + 1) if isinstance(i, int) else bass.ds(i, 1)
                act.activation(oAT[:, 0, at, :].rearrange("p a t -> p (a t)"), bank(4, T), ACT.Copy).then_inc(aoT_hi, 1)

            with act.Fori(0, PAIRS - 1) as i:
                attention(i, W_A)
            attention(PAIRS - 1, W_R)

            def retention(i, n_next):
                for s in range(CH):
                    high(Q_RET + 1 + 3 * i, s, W_R)
                act.wait_ge(chunk_used, CH * (Q_RET + 1 + 3 * i))
                act.activation(qkR.rearrange("p a t -> p (a t)"), bank(0), ACT.Copy).then_inc(rqk_ev, 1)
                act.wait_ge(roT_done, i + 1)
                act.activation(oRT[:, 0, bass.ds(2 * i, 2), :].rearrange("p a t -> p (a t)"), bank(5),
                               ACT.Copy).then_inc(roT_hi, 1)
                for s in range(CH):
                    high(Q_RET + 2 + 3 * i, s, W_R)
                act.wait_ge(chunk_used, CH * (Q_RET + 2 + 3 * i))
                act.activation(vR.rearrange("p a t -> p (a t)"), bank(1), ACT.Copy).then_inc(rv_ev, 1)
                for s in range(CH):
                    if s == CH - 1:
                        act.wait_ge(chunk_used, CH * (Q_RET + 3 + 3 * i))
                        act.activation(swish.rearrange("p a t -> p (a t)"), bank(2), ACT.Silu).then_inc(r_swish, 1)
                    high(Q_RET + 3 + 3 * i, s, n_next)

            with act.Fori(0, RET_HEADS - 1) as i:
                retention(i, W_R)
            retention(RET_HEADS - 1, W_G)

            for q in range(GI):
                for s in range(CH):
                    high(Q_GATE + 1 + q, s, W_G if q < GI - 1 else W_B)
                act.wait_ge(chunk_used, CH * (Q_GATE + 1 + q))
                for a, dst in ((0, gateA), (1, gateR)):
                    act.activation(dst[:, 2 * q:2 * q + 2, :].rearrange("p c t -> p (c t)"), bank(2 * (q % 2) + a),
                                   ACT.Sigmoid).then_inc(g_ready, 1)
                if q == 0:
                    act.wait_ge(roT_done, RET_HEADS + 1)
                    act.activation(oRT[:, 0, 0:2, :].rearrange("p a t -> p (a t)"), bank(5), ACT.Copy).then_inc(roT_hi, 1)
            for Q in (Q_WRET, Q_WRET + 1, Q_OUT):
                for s in range(CH):
                    high(Q, s, W_B)
            for b in range(KT // 2):
                act.wait_ge(b_sum, b + 1)
                act.activation(hT[:, 0, 2 * b:2 * b + 2, :], merged[:, 2 * b:2 * b + 2, :], ACT.Copy).then_inc(b_hi, 1)
            for s in range(CH):
                high(Q_OUT + 1, s, W_B)

            def squares(n):
                for t in range(TT):
                    act.wait_ge(sq_done, TT * n + t)
                    if n == 1 and t == TT - 1:
                        act.wait_ge(chunk_used, CH * QUADS)
                    else:
                        act.wait_ge(stream_done, (TT - 1) * (n - 1) + t + 1)
                    act.activation(junk, banks(4 + 2 * t), ACT.Square, accum_out=ss[:, n, t:t + 1]).then_inc(sq_done, 1)

            squares(1)
            for t in range(TT):
                act.wait_ge(hT_psum, 2 * TT + 2 * t + 1)
                act.activation(h2T[:, 0:4, t * P:(t + 1) * P], ps[:, 2 * t, :].rearrange("p (k t) -> p k t", k=4),
                               ACT.Copy).then_inc(hT_act, 1)
            for t in range(TT):
                act.wait_ge(d_route, 1)
                act.activation(ra[:, t, 0:N_GROUPS], ra[:, t, 0:N_GROUPS], ACT.Exp,
                               accum_out=r1[:, 2, t:t + 1]).then_inc(gexp, 1)
            act.wait_ge(d_route, 2)
            act.activation(r1[:, 6, :], r1[:, 5, :], ACT.Exp).then_inc(e2exp, 1)

            act.wait_ge(sched_ready, 1)
            with act.Fori(0, NP) as p:
                R = act.value_load(sched[0:1, 0, bass.ds(p, 1)], min_val=1, max_val=ROUNDS)
                C = act.value_load(sched[0:1, 1, bass.ds(p, 1)], min_val=0, max_val=ROUNDS * NP)
                with act.Fori(0, R) as r:
                    n = C + r
                    act.wait_ge(gather_lo, n + 1)
                    act.activation(xg[:, 0:4, :].rearrange("p k s -> p (k s)"), bank(0), ACT.Copy).then_inc(xg_act, 1)
                    act.wait_ge(gate_done, n + 1)
                    act.activation(sg, bank(2), ACT.Silu).then_inc(silu_done, 1)
                    act.wait_ge(hidT_done, n + 1)
                    act.activation(hidT.rearrange("p f s -> p (f s)"), bank(0), ACT.Copy).then_inc(hidT_ev, 1)
                    for h in range(2):
                        act.wait_ge(down_done[h], n + 1)
                        act.activation(yS[:, h * HALF:(h + 1) * HALF], bank(2 + h), ACT.Copy).then_inc(yS_ev[h], 1)
            squares(2)

        @block.vector
        def _(dve):
            link, _n = chain(dve, dve_chain, 0)

            def low(Q, s, n):
                dve.wait_ge(hi_ready, CH * Q + s + 1)
                dve.tensor_tensor(split[:, s, 1, 0:n], raw(s, n), split[:, s, 0, 0:n].bitcast(F32),
                                  ALU.subtract).then_inc(lo_ready, 1)

            def mean_square(n):
                for t in range(TT):
                    dve.wait_ge(sq_done, TT * n + t + 1)
                    dve.tensor_scalar(ms[:, n, t:t + 1], ss[:, n, t:t + 1], 1.0 / D, EPS, ALU.mult,
                                      ALU.add).then_inc(ms_done, 1)

            def permuted(ap):
                return ap.rearrange("q (p k) -> q k p", k=KT)

            for j in range(2):
                link(dve.memset(slope[:, j:j + 1], 2.0 ** (-8.0 * (j + 1) / HEADS)))
            for j in range(2):
                dve.memset(qT[(1 - j) * HEAD_DIM:(2 - j) * HEAD_DIM, j], 0.0).then_inc(zeros_ready, 1)
            dve.sem_inc(aoT_lo, 1)
            dve.sem_inc(roT_lo, 1)

            mean_square(0)
            dve.wait_ge(s_gain, 16)
            for t in range(TT):
                dve.wait_ge(rstd_done, t + 1)
                dve.scalar_tensor_tensor(hn[:, t, :, :], permuted(xs[:, t, :]), rstd[:, 0, t:t + 1], permuted(gain[:, :]),
                                         ALU.mult, ALU.mult).then_inc(hn_done, 1)

            def transposed_low(t):
                for h in range(2):
                    b = 2 * t + h
                    dve.wait_ge(hT_act, b + 1)
                    steps, tokens = slice(4 * h, 4 * h + 4), slice(t * P, (t + 1) * P)
                    dve.tensor_tensor(hT[:, 1, steps, tokens], ps[:, b, :].rearrange("p (k t) -> p k t", k=4),
                                      hT[:, 0, steps, tokens].bitcast(F32), ALU.subtract).then_inc(hT_dve, 1)

            low(0, 0, W_A)
            low(0, 1, W_A)
            transposed_low(0)
            transposed_low(1)
            low(0, 2, W_A)
            low(0, 3, W_A)

            dve.wait_ge(const_ready, 3)
            link(dve.tensor_copy(dist, dist_i))
            for g, (window, dil) in enumerate(GROUPS):
                link(dve.tensor_single_scalar(resid_i, dist_i, dil - 1, ALU.bitwise_and))
                link(dve.tensor_copy(resid_f, resid_i))
                link(dve.scalar_tensor_tensor(bias_t[:, g, :], resid_f, MASKED, dist, ALU.mult, ALU.add))
                for cmp, lim in ((ALU.is_gt, 0.0), (ALU.is_lt, float(-window))):
                    if lim <= -T:
                        continue
                    link(dve.tensor_single_scalar(resid_f, dist, lim, cmp))
                    link(dve.scalar_tensor_tensor(bias_t[:, g, :], resid_f, MASKED, bias_t[:, g, :],
                                                  ALU.mult, ALU.add))

            def attention(i, n_next):
                for s in range(CH):
                    low(3 * i + 1, s, W_A)
                for s in range(CH):
                    if s == 2:
                        dve.wait_ge(chunk_used, CH * (3 * i + 2))
                        dve.tensor_copy(kT.rearrange("p g t -> p (g t)"), banks(2, NG * T)).then_inc(ak_ev, 1)
                    low(3 * i + 2, s, W_A)

                def normalise(u):
                    dve.wait_ge(ap_ready, 4 * i + u + 1)
                    dve.reciprocal(rden[:, u:u + 1], den[:, u:u + 1]).then_inc(ap_rden, 1)
                    dve.wait_ge(ap_rden, 4 * i + u + 1)
                    dve.tensor_scalar(probs[u], probs[u], rden[:, u:u + 1], None, ALU.mult).then_inc(ap_norm, 1)

                for u in range(4):
                    span = T if u % 2 == 0 else P
                    dve.wait_ge(as_done, 4 * i + u + 1)
                    dve.scalar_tensor_tensor(probs[u].rearrange("p (g s) -> p g s", g=NG),
                                             bias_t[:, :, T - span:T], slope[:, u // 2:u // 2 + 1],
                                             s_cols(u).rearrange("p (g s) -> p g s", g=NG),
                                             ALU.mult, ALU.add).then_inc(as_chain, 1)
                    dve.wait_ge(as_chain, 4 * i + u + 1)
                    dve.tensor_reduce(negmax[:, u:u + 1], probs[u], AX_X, ALU.max, negate=True).then_inc(as_ready, 1)
                    if u == 2:
                        normalise(0)
                for u in range(1, 4):
                    normalise(u)
                dve.tensor_scalar(slope[:, :], slope[:, :], 2.0 ** (-16.0 / HEADS), None, ALU.mult).then_inc(slope_chain, 1)
                dve.wait_ge(chunk_used, CH * (3 * i + 3))
                dve.tensor_copy(vA.rearrange("p a g n -> p a (g n)"), ps[:, 0:2, 0:NG * P]).then_inc(av_ev, 1)
                for n, u in enumerate((1, 3)):
                    dve.wait_ge(apt_done, 4 * i + 2 + n + 1)
                    dve.tensor_copy(probsT[u], s_cols(u)).then_inc(apt_dve, 1)
                for s in range(CH):
                    low(3 * i + 3, s, n_next)
                dve.wait_ge(aoT_hi, i + 1)
                at = slice(i, i + 1) if isinstance(i, int) else bass.ds(i, 1)
                dve.tensor_tensor(oAT[:, 1, at, :].rearrange("p a t -> p (a t)"), bank(4, T),
                                  oAT[:, 0, at, :].bitcast(F32).rearrange("p a t -> p (a t)"),
                                  ALU.subtract).then_inc(aoT_lo, 1)
                dve.wait_ge(slope_chain, i + 1)

            with dve.Fori(0, PAIRS - 1) as i:
                attention(i, W_A)
            attention(PAIRS - 1, W_R)
            dve.memset(oR, 0.0).then_inc(r_out, 1)
            dve.wait_ge(decay_done, RET_HEADS)

            def retention(i, n_next):
                for s in range(CH):
                    low(Q_RET + 1 + 3 * i, s, W_R)
                dve.wait_ge(roT_hi, i + 1)
                dve.tensor_tensor(oRT[:, 1, bass.ds(2 * i, 2), :].rearrange("p a t -> p (a t)"), bank(5),
                                  oRT[:, 0, bass.ds(2 * i, 2), :].bitcast(F32).rearrange("p a t -> p (a t)"),
                                  ALU.subtract).then_inc(roT_lo, 1)
                for s in range(CH):
                    low(Q_RET + 2 + 3 * i, s, W_R)
                dve.wait_ge(rat_done, i + 1)
                for c, n in ((0, T), (T, P)):
                    ins = dve.scalar_tensor_tensor(attR[:, c:c + n], ps[:, 3, c:c + n], float(RK) ** -0.5,
                                                   decay[:, bass.ds(i, 1), 0:n].rearrange("p a n -> p (a n)"),
                                                   ALU.mult, ALU.mult)
                ins.then_inc(rat_ev, 1)
                for s in range(2):
                    low(Q_RET + 3 + 3 * i, s, n_next)
                dve.wait_ge(ry_done, i + 1)
                for t in range(TT):
                    dve.bn_stats(stats[:, t, :], ps[:, 4, t * RV:(t + 1) * RV]).then_inc(r_stats, 1)
                dve.wait_ge(r_stats, TT * i + TT)
                dve.tensor_copy(gap[:, :], half_neg[:, :]).then_inc(r_gap, 1)
                for t in range(TT):
                    dve.bn_aggr(meanvar[:, t, :], stats[:, t, :]).then_inc(r_aggr, 1)
                dve.wait_ge(r_aggr, TT * i + TT)
                dve.tensor_scalar(meanvar[:, :, 1], meanvar[:, :, 1], EPS, None, ALU.add).then_inc(rvar, 1)
                low(Q_RET + 3 + 3 * i, 2, n_next)
                dve.wait_ge(rrstd, i + 1)
                for t in range(TT):
                    ins = dve.tensor_scalar(oR[:, t, :], ps[:, 4, t * RV:(t + 1) * RV], meanvar[:, t, 0:1],
                                            rstdR[:, t:t + 1], ALU.subtract, ALU.mult)
                ins.then_inc(r_norm, 1)
                dve.wait_ge(r_norm, i + 1)
                dve.wait_ge(r_swish, i + 1)
                dve.tensor_tensor(oR, oR, swish, ALU.mult).then_inc(r_out, 1)
                low(Q_RET + 3 + 3 * i, 3, n_next)

            with dve.Fori(0, RET_HEADS - 1) as i:
                retention(i, W_R)
            retention(RET_HEADS - 1, W_G)
            for q in range(GI):
                for s in range(CH):
                    low(Q_GATE + 1 + q, s, W_G if q < GI - 1 else W_B)
                if q == 0:
                    dve.wait_ge(roT_hi, RET_HEADS + 1)
                    dve.tensor_tensor(oRT[:, 1, 0:2, :].rearrange("p a t -> p (a t)"), bank(5),
                                      oRT[:, 0, 0:2, :].bitcast(F32).rearrange("p a t -> p (a t)"),
                                      ALU.subtract).then_inc(roT_lo, 1)

            for s in range(CH):
                low(Q_WRET, s, W_B)
            dve.wait_ge(g_ready, 2 * GI)
            for b in range(KT // 2):
                if b < KT // 2 - 1:
                    dve.wait_ge(bA_done, b + 1)
                else:
                    dve.wait_ge(chunk_used, CH * (Q_ATTN + 1))
                dve.tensor_tensor(merged[:, 2 * b:2 * b + 2, :], ps[:, 4 + b, :].rearrange("p (c t) -> p c t", c=2),
                                  gateA[:, 2 * b:2 * b + 2, :], ALU.mult).then_inc(bA_ev, 1)
            for s in range(CH):
                low(Q_WRET + 1, s, W_B)
            for s in range(CH - 1):
                low(Q_OUT, s, W_B)
            dve.wait_ge(bA_ev, KT // 2)
            for b in range(KT // 2):
                tiles = slice(2 * b, 2 * b + 2)
                if b < KT // 2 - 1:
                    dve.wait_ge(bR_done, b + 1)
                else:
                    dve.wait_ge(chunk_used, CH * (Q_WRET + 2))
                dve.tensor_tensor(mtmp, ps[:, b, :].rearrange("p (c t) -> p c t", c=2), gateR[:, tiles, :],
                                  ALU.mult).then_inc(b_tmp, 1)
                dve.wait_ge(b_tmp, b + 1)
                dve.tensor_tensor(merged[:, tiles, :], merged[:, tiles, :], mtmp, ALU.add).then_inc(b_sum, 1)
                if b == 0:
                    low(Q_OUT, CH - 1, W_B)
                dve.wait_ge(b_hi, b + 1)
                dve.tensor_tensor(hT[:, 1, tiles, :], merged[:, tiles, :], hT[:, 0, tiles, :].bitcast(F32),
                                  ALU.subtract).then_inc(b_ready, 1)
            for s in range(CH):
                low(Q_OUT + 1, s, W_B)

            mean_square(1)
            dve.wait_ge(s_gain, 32)
            for t in range(TT):
                dve.wait_ge(rstd_done, TT + t + 1)
                dve.scalar_tensor_tensor(hn[:, t, :, :], permuted(banks(4 + 2 * t)), rstd[:, 1, t:t + 1],
                                         permuted(gain[:, :]), ALU.mult, ALU.mult).then_inc(hn_done, 1)
            dve.memset(gatedT[:, :], 0.0).then_inc(pgt_ev, 1)
            for t in range(TT):
                dve.wait_ge(hT_psum, 2 * TT + 2 * t + 2)
                dve.tensor_copy(h2T[:, 4:8, t * P:(t + 1) * P],
                                ps[:, 2 * t + 1, :].rearrange("p (k t) -> p k t", k=4)).then_inc(hT_dve, 1)
            for h in range(2):
                dve.memset(yS[:, h * HALF:(h + 1) * HALF], 0.0).then_inc(yS_ev[h], 1)
            dve.wait_ge(s_wr, 32)
            dve.wait_ge(logits_done, 1)
            dve.wait_ge(const_ready, 7)

            def per_row(k, n):
                return r1[:, k, :].unsqueeze(2).to_broadcast([P, TT, n])

            lp = ps[:, 0, 0:TT * 64].rearrange("p (a n) -> p a n", a=TT)[:, :, 0:NR]
            link(dve.tensor_tensor(lg[:, :, :], lp, br[:, :].unsqueeze(1).to_broadcast([P, TT, NR]), ALU.add))
            gl, el = lg[:, :, 0:N_GROUPS], lg[:, :, N_GROUPS:NR]
            rga, rgb = ra[:, :, 0:N_GROUPS], rb[:, :, 0:N_GROUPS]
            link(dve.tensor_reduce(r1[:, 0, :], gl, AX_X, ALU.max))
            link(dve.tensor_tensor(rb[:, :, 0:N_GROUPS], gl, per_row(0, N_GROUPS), ALU.is_equal))
            dve.tensor_tensor(rga, gl, per_row(0, N_GROUPS), ALU.subtract).then_inc(d_route, 1)

            def first_of(hits, n, k, dst):
                ids = rev_ids[:, 0:n].unsqueeze(1).to_broadcast([P, TT, n])
                link(dve.tensor_tensor(hits, hits, ids, ALU.mult))
                link(dve.tensor_reduce(r1[:, k, :], hits, AX_X, ALU.max))
                link(dve.tensor_tensor(dst, hits, per_row(k, n), ALU.is_equal))

            first_of(rgb, N_GROUPS, 1, rgb)
            link(dve.tensor_scalar(rgb, rgb, 1.0, -MASKED, ALU.subtract, ALU.mult))
            el_g = el.rearrange("p a (g n) -> p a g n", g=N_GROUPS)
            link(dve.tensor_tensor(el_g, el_g, rgb.unsqueeze(3).to_broadcast([P, TT, N_GROUPS, PER_GROUP]), ALU.add))
            rbe = rb[:, :, N_GROUPS:NR]
            link(dve.tensor_reduce(r1[:, 3, :], el, AX_X, ALU.max))
            link(dve.tensor_tensor(rbe, el, per_row(3, E), ALU.is_equal))
            first_of(rbe, E, 7, oh1[:, :, :])
            link(dve.scalar_tensor_tensor(el, oh1[:, :, :], 2 * MASKED, el, ALU.mult, ALU.add))
            link(dve.tensor_reduce(r1[:, 4, :], el, AX_X, ALU.max))
            link(dve.tensor_tensor(rbe, el, per_row(4, E), ALU.is_equal))
            first_of(rbe, E, 8, oh2[:, :, :])
            dve.tensor_tensor(r1[:, 5, :], r1[:, 4, :], r1[:, 3, :], ALU.subtract).then_inc(d_route, 1)
            link(dve.tensor_tensor(sel[:, :, :], oh1[:, :, :], oh2[:, :, :], ALU.add))
            dve.tensor_tensor(sel_all[:, :], sel[:, 0, :], sel[:, 1, :], ALU.add).then_inc(sel_ready, 1)
            dve.wait_ge(gexp, TT)
            dve.wait_ge(e2exp, 1)
            link(dve.tensor_scalar(r1[:, 9, :], r1[:, 6, :], 1.0, None, ALU.add))
            link(dve.tensor_tensor(r1[:, 9, :], r1[:, 9, :], r1[:, 2, :], ALU.mult))
            dve.wait_ge(cnt_done, 1)
            link(dve.tensor_scalar(fuller[:, :], ps[0:NP, 2, 0:1], 1.0, None, ALU.max))
            link(dve.tensor_tensor(fuller[:, :], fuller[:, :], ps[0:NP, 2, 1:2], ALU.max))
            link(dve.tensor_scalar(begun[:, :], slot_ids[0:NP, 0:ROUNDS * SLOTS:SLOTS], fuller[:, 0:1], None, ALU.is_le))
            dve.tensor_reduce(rounds[:, :], begun[:, :], AX_X, ALU.add).then_inc(rounds_ready, 1)
            link(dve.reciprocal(r1[:, 10, :], r1[:, 9, :]))
            link(dve.tensor_tensor(r1[:, 11, :], r1[:, 10, :], r1[:, 6, :], ALU.mult))
            dve.tensor_tensor(oh1[:, :, :], oh1[:, :, :], per_row(10, E), ALU.mult).then_inc(weighted, 1)
            dve.wait_ge(sched_psum, 1)
            dve.tensor_copy(sched[:, :, :].rearrange("p a n -> p (a n)"), ps[0:1, 3, 0:2 * NP]).then_inc(sched_ready, 1)
            link(dve.tensor_tensor(oh2[:, :, :], oh2[:, :, :], per_row(11, E), ALU.mult))
            dve.wait_ge(weighted, 1)
            dve.tensor_tensor(gate[:, :, :], oh1[:, :, :], oh2[:, :, :], ALU.add).then_inc(weighted, 1)
            dve.wait_ge(pos_done, 1)
            pp = ps[:, 1, 0:TT * E].rearrange("p (a n) -> p a n", a=TT)
            dve.scalar_tensor_tensor(pos[:, :, :], pp, 1.0, sel[:, :, :], ALU.add, ALU.mult).then_inc(weighted, 1)
            dve.wait_ge(sched_ready, 1)
            with dve.Fori(0, NP) as p:
                R = dve.value_load(sched[0:1, 0, bass.ds(p, 1)], min_val=1, max_val=ROUNDS)
                C = dve.value_load(sched[0:1, 1, bass.ds(p, 1)], min_val=0, max_val=ROUNDS * NP)
                with dve.Fori(0, R) as r:
                    n = C + r
                    ids = slot_ids[:, bass.ds(r * SLOTS, SLOTS)]

                    def each(table, t):
                        return table[:, t, bass.ds(2 * p, 2)].unsqueeze(2).to_broadcast([P, 2, SLOTS])

                    dve.wait_ge(weighted, 3)
                    for t in range(TT):
                        dve.tensor_tensor(onehot[:, t, :].rearrange("p (j s) -> p j s", j=2),
                                          ids.unsqueeze(1).to_broadcast([P, 2, SLOTS]), each(pos, t),
                                          ALU.is_equal).then_inc(P_built, 1)
                    dve.wait_ge(P_built, TT * n + TT)
                    for t in range(TT):
                        dve.tensor_tensor(gated[:, t, :].rearrange("p (j s) -> p j s", j=2),
                                          onehot[:, t, :].rearrange("p (j s) -> p j s", j=2), each(gate, t),
                                          ALU.mult).then_inc(Pg_built, 1)
                    dve.wait_ge(gather_hi, n + 1)
                    dve.tensor_copy(xg[:, 4:8, :].rearrange("p k s -> p (k s)"), bank(1)).then_inc(xg_dve, 1)
                    dve.wait_ge(silu_done, n + 1)
                    dve.wait_ge(up_done, n + 1)
                    dve.tensor_tensor(hid, sg, bank(3), ALU.mult).then_inc(hid_ready, 1)
                    dve.wait_ge(pgt_done, n + 1)
                    dve.tensor_copy(gatedT[:, :], bank(1, T)).then_inc(pgt_ev, 1)

            mean_square(2)
            dve.wait_ge(s_gain, 48)
            for t in range(TT):
                dve.wait_ge(rstd_done, 2 * TT + t + 1)
                for h in range(2):
                    cols = slice(h * HALF, (h + 1) * HALF)
                    dve.scalar_tensor_tensor(res[:, t, cols], bank(4 + 2 * t + h), rstd[:, 2, t:t + 1], gain[:, cols],
                                             ALU.mult, ALU.mult).then_inc(fin, 1)

        @block.tensor
        def _(pe):
            def mm(o, l, r, start, stop, shared=False):
                return pe.matmul(o, lhsT=l, rhs=r, start=start, stop=stop, skip_group_check=shared)

            def mm3(o, l, r, start):
                mm(o, l[0], r[0], start, False, True)
                mm(o, l[0], r[1], False, False, True)
                return mm(o, l[1], r[0], False, False, True)

            def transpose_rows(n):
                for t in range(TT):
                    pe.wait_ge(hn_done, TT * n + t + 1)
                    for k in range(KT):
                        ins = pe.transpose(ps[:, 2 * t + k // 4, (k % 4) * P:(k % 4 + 1) * P], hn[:, t, k, :],
                                           ident[:, :])
                        if k in (3, 7):
                            ins.then_inc(hT_psum, 1)

            def quad(Q, n, steps, use, chunks=range(CH)):
                for s in chunks:
                    pe.wait_ge(lo_ready, CH * Q + s + 1)
                    ins = use(s, parts(s, n, steps))
                    ins.then_inc(chunk_used, 1)

            def columns(n_tiles, b, w_words):
                def use(s, w):
                    for kk in range(2):
                        k = 2 * s + kk
                        for c in range(n_tiles):
                            o = ps[:, b + c // 2, (c % 2) * T:(c % 2 + 1) * T]
                            ins = mm3(o, [w[a][:, kk, c * P:(c + 1) * P] for a in range(2)],
                                      [hT[:, a, k, :] for a in range(2)], k == 0 and c % 2 == 0)
                    return ins
                return use

            def rows(outs, own_bank):
                def use(s, w):
                    for kk in range(2):
                        k = 2 * s + kk
                        for t in range(TT):
                            ins = mm3(outs[t], [hT[:, a, k, t * P:(t + 1) * P] for a in range(2)],
                                      [w[a][:, kk, :] for a in range(2)], k == 0 and (own_bank or t == 0))
                    return ins
                return use

            pe.wait_ge(const_ready, 1)
            transpose_rows(0)
            pe.wait_ge(hT_dve, 2 * TT - 1)

            pe.wait_ge(zeros_ready, 2)
            with pe.Fori(0, PAIRS) as i:
                queries = columns(NG, 0, W_A)
                quad(3 * i, W_A, 2, queries, range(2))
                pe.wait_ge(hT_dve, 2 * TT)
                quad(3 * i, W_A, 2, queries, range(2, CH))
                quad(3 * i + 1, W_A, 2, columns(NG, 2, W_A))
                pe.wait_ge(aq_ev, 2 * i + 2)
                values = rows([bank(0, NG * P), bank(1, NG * P)], True)
                quad(3 * i + 2, W_A, 2, values, range(1))
                pe.wait_ge(ak_ev, i + 1)
                pe.wait_ge(aoT_lo, i + 1)
                for u in range(4):
                    j, t = u // 2, 1 - u % 2
                    span = (t + 1) * P
                    for g in range(NG):
                        ins = mm(s_cols(u)[:, g * span:(g + 1) * span], qT[:, j, g, t * P:(t + 1) * P],
                                 kT[:, g, 0:span], True, True)
                    ins.then_inc(as_done, 1)
                quad(3 * i + 2, W_A, 2, values, range(1, CH))
                for u, normed in ((0, 1), (2, 3), (1, 3), (3, 4)):
                    pe.wait_ge(ap_norm, 4 * i + normed)
                    for c in range(UC[u % 2] // P):
                        ins = pe.transpose(s_cols(u)[:, c * P:(c + 1) * P], probs[u][:, c * P:(c + 1) * P], ident[:, :])
                    ins.then_inc(apt_done, 1)
                pe.wait_ge(av_ev, i + 1)
                pe.wait_ge(apt_act, 2 * i + 2)
                for t in (1, 0):
                    if t == 0:
                        pe.wait_ge(apt_dve, 2 * i + 2)
                    n_blocks = UC[1 - t] // P
                    for c in range(n_blocks):
                        g, s = c // (t + 1), c % (t + 1)
                        for j in range(2):
                            ins = mm(ps[j * HEAD_DIM:(j + 1) * HEAD_DIM, 4, t * P:(t + 1) * P],
                                     vA[:, s, g, j * HEAD_DIM:(j + 1) * HEAD_DIM],
                                     probsT[2 * j + 1 - t][:, c * P:(c + 1) * P], c == 0, c == n_blocks - 1)
                ins.then_inc(aoT_done, 1)

            def transpose_ret(i):
                pe.wait_ge(r_out, i + 1)
                pe.wait_ge(roT_lo, i + 1)
                for c in range(2):
                    for t in range(TT):
                        ins = pe.transpose(ps[:, 5, c * T + t * P:c * T + (t + 1) * P], oR[:, t, c * P:(c + 1) * P],
                                           ident[:, :])
                ins.then_inc(roT_done, 1)

            with pe.Fori(0, RET_HEADS) as i:
                quad(Q_RET + 3 * i, W_R, 2, columns(2, 0, W_R))
                transpose_ret(i)
                quad(Q_RET + 1 + 3 * i, W_R, 2, rows([ps[:, 1, t * RV:(t + 1) * RV] for t in range(TT)], False))
                pe.wait_ge(rqk_ev, i + 1)
                mm(ps[:, 3, 0:T], qkR[:, 1, 0:P], qkR[:, 0, :], True, True)
                mm(ps[:, 3, T:T + P], qkR[:, 1, P:T], qkR[:, 0, P:T], True, True).then_inc(rat_done, 1)
                swish_gate = rows([ps[:, 2, t * RV:(t + 1) * RV] for t in range(TT)], False)
                quad(Q_RET + 2 + 3 * i, W_R, 2, swish_gate, range(2))
                pe.wait_ge(rat_ev, i + 1)
                pe.wait_ge(rv_ev, i + 1)
                mm(ps[:, 4, 0:RV], attR[:, 0:P], vR[:, 0, :], True, True)
                mm(ps[:, 4, RV:2 * RV], attR[:, P:2 * P], vR[:, 0, :], True, False)
                mm(ps[:, 4, RV:2 * RV], attR[:, 2 * P:3 * P], vR[:, 1, :], False, True).then_inc(ry_done, 1)
                quad(Q_RET + 2 + 3 * i, W_R, 2, swish_gate, range(2, CH))

            quad(Q_GATE, W_G, 2, columns(4, 0, W_G))
            transpose_ret(RET_HEADS)
            quad(Q_GATE + 1, W_G, 2, columns(4, 2, W_G))
            with pe.Fori(1, GI // 2) as i:
                for m in range(2):
                    pe.wait_ge(g_ready, 4 * i - 2 + 2 * m)
                    quad(Q_GATE + m + 2 * i, W_G, 2, columns(4, 2 * m, W_G))

            def branch(outs_from, c0, tile_of, oT, n_c, done):
                def use(s, w):
                    c = c0 + s
                    for j in range(KT):
                        ins = mm3(ps[:, outs_from + j // 2, (j % 2) * T:(j % 2 + 1) * T],
                                  [w[a][:, 0, j * P:(j + 1) * P] for a in range(2)],
                                  [oT[:, a, tile_of(c), :] for a in range(2)], c == 0 and j % 2 == 0)
                        if c == n_c - 1 and j % 2 == 1 and j < KT - 1:
                            ins.then_inc(done, 1)
                    return ins
                return use

            pe.wait_ge(aoT_lo, PAIRS + 1)
            pe.wait_ge(roT_lo, RET_HEADS + 2)
            quad(Q_ATTN, W_B, 1, branch(4, 0, lambda c: c, oAT, PAIRS, bA_done))
            pe.wait_ge(g_ready, 2 * GI)
            for m in range(2):
                quad(Q_WRET + m, W_B, 1, branch(0, CH * m, lambda c: (c + 2) % (2 * RET_HEADS), oRT,
                                                2 * RET_HEADS, bR_done))

            pe.wait_ge(bA_ev, KT // 2)
            for t in range(TT):
                for h in range(2):
                    mm(ps[:, 4 + 2 * t + h, :], ident[:, :], xs[:, t, h * HALF:(h + 1) * HALF], True, False, True)

            def project_out(j0):
                def use(s, w):
                    j = j0 + s
                    pe.wait_ge(b_ready, j // 2 + 1)
                    for t in range(TT):
                        for h in range(2):
                            ins = mm3(ps[:, 4 + 2 * t + h, :], [hT[:, a, j, t * P:(t + 1) * P] for a in range(2)],
                                      [w[a][:, 0, h * HALF:(h + 1) * HALF] for a in range(2)], False)
                        if j == KT - 1 and t == 0:
                            ins.then_inc(stream_done, 1)
                    return ins
                return use

            quad(Q_OUT, W_B, 1, project_out(0))
            quad(Q_OUT + 1, W_B, 1, project_out(CH))

            transpose_rows(1)
            pe.wait_ge(s_wr, 32)
            for t in range(TT):
                pe.wait_ge(hT_act, 2 * TT + t + 1)
                pe.wait_ge(hT_dve, 2 * TT + t + 1)
                for k in range(KT):
                    ins = mm(ps[:, 0, t * 64:t * 64 + NR], h2T[:, k, t * P:(t + 1) * P], wr[:, k, :], k == 0, k == KT - 1)
            ins.then_inc(logits_done, 1)
            pe.wait_ge(sel_ready, 1)
            pe.wait_ge(const_ready, 7)
            chosen = sel_all[:, :].rearrange("p (n j) -> p j n", j=2)
            for j in range(2):
                ins = mm(ps[0:NP, 2, j:j + 1], chosen[:, j, :], ones[:, 0:1], True, True)
            ins.then_inc(cnt_done, 1)
            mm(ps[:, 1, 0:E], before[:, :], sel[:, 0, :], True, True)
            mm(ps[:, 1, E:2 * E], ones[:, :], sel[:, 0, :], True, False)
            mm(ps[:, 1, E:2 * E], before[:, :], sel[:, 1, :], False, True).then_inc(pos_done, 1)
            pe.wait_ge(rounds_ready, 1)
            mm(ps[0:1, 3, 0:NP], rounds[:, :], ident[0:NP, 0:NP], True, True)
            mm(ps[0:1, 3, NP:2 * NP], rounds[:, :], before[0:NP, 0:NP], True, True).then_inc(sched_psum, 1)

            def scatter(h, t):
                return mm(ps[:, 4 + 2 * t + h, :], gatedT[:, t * P:(t + 1) * P], yS[:, h * HALF:(h + 1) * HALF],
                          False, False, True)

            def both(b, w, steps, left, cols, halfway=None, read={}):
                n_steps = left.shape[1]
                for k in steps:
                    if halfway is not None and k == n_steps // 2:
                        pe.wait_ge(halfway, 32)
                    if k in read:
                        ins.then_inc(read[k], 1)
                    for j in range(2):
                        ins = mm(ps[j * SLOTS:(j + 1) * SLOTS, b, :], left[:, k, j * SLOTS:(j + 1) * SLOTS],
                                 w[j][:, k, cols], k == 0, k == n_steps - 1)
                return ins

            pe.wait_ge(sched_ready, 1)
            def experts(p, m, i):
                at = bass.ds(p, 1) if not isinstance(p, int) else slice(p, p + 1)
                R = pe.value_load(sched[0:1, 0, at], min_val=1, max_val=ROUNDS)
                C = pe.value_load(sched[0:1, 1, at], min_val=0, max_val=ROUNDS * NP)
                tiles = [slots[s] for s in tiles_of(m)]
                scatter_early = m > 0 or isinstance(p, int)
                w_gate, w_up = ([w.rearrange("p (k n) -> p k n", k=KT) for w in tiles[a:a + 2]] for a in (0, 2))
                w_down = [w.rearrange("p (c n) -> p c n", c=FT) for w in tiles[4:6]]

                def wait_tiles(*which):
                    for j in which:
                        pe.wait_ge(slot_loaded[tiles_of(m)[j]], 16 * (6 * CYCLE // SLOT_N) * i + 16 * loads_of(m, j))

                with pe.Fori(0, R) as r:
                    n = C + r
                    pe.wait_ge(P_built, TT * n + TT)
                    pe.wait_ge(pgt_ev, n + 1)
                    for k in range(KT):
                        for t in range(TT):
                            ins = mm(ps[:, k // 4, (k % 4) * P:(k % 4 + 1) * P], hn[:, t, k, :], onehot[:, t, :],
                                     t == 0, t == TT - 1)
                        if k in (3, 7):
                            ins.then_inc(gather_lo if k == 3 else gather_hi, 1)
                    pe.wait_ge(yS_ev[0], n + 1)
                    scatter(0, 0)
                    pe.wait_ge(xg_act, n + 1)
                    pe.wait_ge(xg_dve, n + 1)
                    wait_tiles(0, 1)
                    both(2, w_gate, range(KT), xg, slice(0, FF), second_gate if isinstance(p, int) else None,
                         {KT // 4: gate_quarter, KT // 2: gate_half}).then_inc(gate_done, 1)
                    pe.wait_ge(yS_ev[1], n + 1)
                    if scatter_early:
                        scatter(0, 1)
                        scatter(1, 0)
                    wait_tiles(2, 3)
                    both(3, w_up, range(KT), xg, slice(0, FF), second_up if isinstance(p, int) else None).then_inc(up_done, 1)
                    if not scatter_early:
                        scatter(0, 1)
                        scatter(1, 0)
                    scatter(1, 1)
                    pe.wait_ge(hid_ready, n + 1)
                    for f in range(FT):
                        ins = pe.transpose(ps[:, 0, f * P:(f + 1) * P], hid[:, f * P:(f + 1) * P], ident[:, :])
                    ins.then_inc(hidT_done, 1)
                    pe.wait_ge(Pg_built, TT * n + TT)
                    for t in range(TT):
                        ins = pe.transpose(ps[:, 1, t * P:(t + 1) * P], gated[:, t, :], ident[:, :])
                    ins.then_inc(pgt_done, 1)
                    pe.wait_ge(hidT_ev, n + 1)
                    for j in (4, 5):
                        pe.wait_ge(first_down[tiles_of(m)[j]], 32 * i + 32)
                    if isinstance(p, int):
                        wait_tiles(4, 5)
                        for h in range(2):
                            if h == 1:
                                pe.wait_ge(second_down, 32)
                            both(2 + h, w_down, range(FT), hidT, slice(h * HALF, (h + 1) * HALF),
                                 last_down if h else None).then_inc(down_done[h], 1)
                    else:
                        for h in range(2):
                            both(2 + h, w_down, range(FT // 2), hidT, slice(h * HALF, (h + 1) * HALF))
                        wait_tiles(4, 5)
                        for h in range(2):
                            both(2 + h, w_down, range(FT // 2, FT), hidT,
                                 slice(h * HALF, (h + 1) * HALF)).then_inc(down_done[h], 1)

            pe.wait_ge(early, 16 * 3 * RET_HEADS)
            with pe.Fori(0, NP // CYCLE) as i:
                for m in range(CYCLE):
                    experts(CYCLE * i + m, m, i)
            experts(NP - 1, 0, NP // CYCLE)
            CL = pe.value_load(sched[0:1, 1, NP - 1:NP], min_val=0, max_val=ROUNDS * NP)
            RL = pe.value_load(sched[0:1, 0, NP - 1:NP], min_val=1, max_val=ROUNDS)
            n = CL + RL
            pe.wait_ge(pgt_ev, n + 1)
            pe.wait_ge(yS_ev[0], n + 1)
            for t in range(TT):
                scatter(0, t)
            pe.wait_ge(yS_ev[1], n + 1)
            for t in range(TT):
                scatter(1, t).then_inc(stream_done, 1)


_OUT = (1, 256, 1024)


def kernel(x, g_mix, w_in, w_attn_branch, w_ret_branch, w_out, g_ffn, w_group_router, b_group_router,
           w_expert_router, b_expert_router, w_gate, w_up, w_down, g_final):
    import concourse.bacc as _bacc
    from concourse.bass_utils import run_bass_kernel_spmd as _run

    nc = _bacc.Bacc("TRN2", target_bir_lowering=False, num_devices=1)
    given = {
        "x": np.asarray(x)[0],
        "g_mix": np.asarray(g_mix)[0],
        "w_in": np.asarray(w_in)[0],
        "w_attn": np.asarray(w_attn_branch)[0],
        "w_ret": np.asarray(w_ret_branch)[0],
        "w_out": np.asarray(w_out)[0],
        "g_ffn": np.asarray(g_ffn)[0],
        "w_router": np.concatenate([np.asarray(w_group_router)[0], np.asarray(w_expert_router)[0]], axis=1),
        "b_router": np.concatenate([np.asarray(b_group_router)[0], np.asarray(b_expert_router)[0]]),
        "w_gate": np.asarray(w_gate)[0],
        "w_up": np.asarray(w_up)[0],
        "w_down": np.asarray(w_down)[0],
        "g_final": np.asarray(g_final),
    }
    arrays = {f"in_{n}": np.ascontiguousarray(a) for n, a in given.items()}
    aps = {n: nc.dram_tensor(f"in_{n}", arrays[f"in_{n}"].shape, mybir.dt.from_np(arrays[f"in_{n}"].dtype),
                             kind="ExternalInput").ap() for n in given}
    out = nc.dram_tensor("out_0", _OUT[1:], F32, kind="ExternalOutput").ap()
    hybrid_block(nc, out=out, **aps)
    r = _run(nc, [arrays], core_ids=[0])
    return r.results[0]["out_0"].reshape(_OUT)
```
